# Optimizing a Trainium2 kernel written in Bass

```python
import math
import jax, jax.numpy as jnp
from jax import lax
import numpy as np

D_MODEL = 1024
BATCH = 1
SEQ = 256
DEPTH = 1

MIX_WIDTH = D_MODEL
HEAD_DIM = 64
RWKV_WIDTH = MIX_WIDTH // 2
RWKV_HEADS = RWKV_WIDTH // HEAD_DIM
MOBA_WIDTH = MIX_WIDTH - RWKV_WIDTH
MOBA_HEADS = MOBA_WIDTH // HEAD_DIM
DECAY_LORA = 64
ICLR_LORA = 64
GATE_LORA = 128
DECAY_SCALE = math.exp(-0.5)
GN_EPS = 64e-5
MOBA_BLOCK = 256
MOBA_TOPK = 3
MOBA_Q_CHUNK = 32
MEM_LEN = 256
XATTN_HEADS = 4
XATTN_HEAD_DIM = D_MODEL // XATTN_HEADS
D_FF = 4 * D_MODEL
NORM_EPS = 1e-6
RWKV_IN = 3 * RWKV_WIDTH + DECAY_LORA + ICLR_LORA + GATE_LORA
MOBA_IN = 3 * MOBA_WIDTH
IN_WIDTH = RWKV_IN + MOBA_IN

kernel_name = "hymba_rwkv7_moba_xattn_sqrelu"

def rms_norm(x, g):
    xf = x.astype(jnp.float32)
    y = xf * lax.rsqrt(jnp.mean(xf * xf, axis=-1, keepdims=True) + NORM_EPS)
    return y * g.astype(jnp.float32)

def rwkv7_time_mix(z, mu, w0, w_up, a0, a_up, g_up, k_k, k_a, r_k, ln_w, ln_b):
    z = z.astype(jnp.float32)
    B, T, _ = z.shape
    H, N = RWKV_HEADS, HEAD_DIM
    z_prev = jnp.pad(z, ((0, 0), (1, 0), (0, 0)))[:, :-1]
    z = z + (z_prev - z) * mu
    r, k, v, wd, ad, gd = jnp.split(
        z, [RWKV_WIDTH, 2 * RWKV_WIDTH, 3 * RWKV_WIDTH,
            3 * RWKV_WIDTH + DECAY_LORA, 3 * RWKV_WIDTH + DECAY_LORA + ICLR_LORA], axis=-1)
    decay = jnp.exp(-DECAY_SCALE * jax.nn.sigmoid(w0 + jnp.tanh(wd) @ w_up))
    a = jax.nn.sigmoid(a0 + ad @ a_up)
    g = jax.nn.sigmoid(gd) @ g_up
    kk = k * k_k
    k = k * (1.0 + (a - 1.0) * k_a)
    hd = lambda t: t.reshape(B, T, H, N)
    r, k, v, decay, a, kk = hd(r), hd(k), hd(v), hd(decay), hd(a), hd(kk)
    kk = kk / jnp.maximum(jnp.sqrt(jnp.sum(kk * kk, axis=-1, keepdims=True)), 1e-12)

    def step(S, inp):
        r_t, w_t, k_t, v_t, kk_t, a_t = inp
        sa = jnp.einsum('bhvk,bhk->bhv', S, -kk_t)
        S = (S * w_t[:, :, None, :] + sa[..., None] * (kk_t * a_t)[:, :, None, :]
             + v_t[..., None] * k_t[:, :, None, :])
        y = jnp.einsum('bhvk,bhk->bhv', S, r_t)
        return S, y

    tm = lambda t: jnp.swapaxes(t, 0, 1)
    S0 = jnp.zeros((B, H, N, N), jnp.float32)
    _, ys = lax.scan(step, S0, (tm(r), tm(decay), tm(k), tm(v), tm(kk), tm(a)))
    y = tm(ys)
    m = jnp.mean(y, axis=-1, keepdims=True)
    var = jnp.mean((y - m) ** 2, axis=-1, keepdims=True)
    y = ((y - m) * lax.rsqrt(var + GN_EPS)).reshape(B, T, RWKV_WIDTH) * ln_w + ln_b
    bonus = jnp.sum(r * k * r_k, axis=-1, keepdims=True) * v
    return (y + bonus.reshape(B, T, RWKV_WIDTH)) * g

def moba_attention(q, k, v):
    B, T, _ = q.shape
    H, D, BLK, QC = MOBA_HEADS, HEAD_DIM, MOBA_BLOCK, MOBA_Q_CHUNK
    Tp = ((T + BLK - 1) // BLK) * BLK
    nb = Tp // BLK
    nc = Tp // QC
    pad = lambda t: jnp.pad(t, ((0, 0), (0, Tp - T), (0, 0))).reshape(B, Tp, H, D).transpose(0, 2, 1, 3)
    q, k, v = pad(q), pad(k), pad(v)
    kb = k.reshape(B, H, nb, BLK, D)
    vb = v.reshape(B, H, nb, BLK, D)
    kmean = jnp.mean(kb.astype(jnp.float32), axis=3)
    gate = jnp.einsum('bhtd,bhnd->bhtn', q.astype(jnp.float32), kmean)
    own = jnp.arange(Tp) // BLK
    past = jnp.arange(nb)[None, :] < own[:, None]
    gate = jnp.where(past, gate, -jnp.inf)
    n_sel = min(MOBA_TOPK, nb)
    _, idx = lax.top_k(gate, n_sel)
    valid = idx < own[None, None, :, None]
    scale = HEAD_DIM ** -0.5
    chunk = lambda t: jnp.moveaxis(t.reshape(B, H, nc, QC, *t.shape[3:]), 2, 0)
    gather = jax.vmap(jax.vmap(lambda t, i: t[i]))

    def attend(args):
        c, q_c, idx_c, val_c = args
        q0 = c * QC
        ob = q0 // BLK
        k_own = lax.dynamic_index_in_dim(kb, ob, axis=2, keepdims=False)
        v_own = lax.dynamic_index_in_dim(vb, ob, axis=2, keepdims=False)
        k_sel = gather(kb, idx_c)
        v_sel = gather(vb, idx_c)
        s_sel = jnp.einsum('bhqd,bhqnkd->bhqnk', q_c, k_sel).astype(jnp.float32) * scale
        s_sel = jnp.where(val_c[..., None], s_sel, -jnp.inf).reshape(B, H, QC, n_sel * BLK)
        s_own = jnp.einsum('bhqd,bhkd->bhqk', q_c, k_own).astype(jnp.float32) * scale
        qpos = q0 + jnp.arange(QC)
        kpos = ob * BLK + jnp.arange(BLK)
        s_own = jnp.where(kpos[None, :] <= qpos[:, None], s_own, -jnp.inf)
        p = jax.nn.softmax(jnp.concatenate([s_sel, s_own], axis=-1), axis=-1)
        p_sel = p[..., :n_sel * BLK].reshape(B, H, QC, n_sel, BLK)
        p_own = p[..., n_sel * BLK:]
        return (jnp.einsum('bhqnk,bhqnkd->bhqd', p_sel, v_sel.astype(jnp.float32))
                + jnp.einsum('bhqk,bhkd->bhqd', p_own, v_own.astype(jnp.float32)))

    outs = lax.map(attend, (jnp.arange(nc), chunk(q), chunk(idx), chunk(valid)))
    out = jnp.moveaxis(outs, 0, 2).reshape(B, H, Tp, D)[:, :, :T]
    return out.transpose(0, 2, 1, 3).reshape(B, T, MOBA_WIDTH)

def memory_cross_attention(u, m, w_q, w_kv, w_o):
    B, T, _ = u.shape
    q = (u @ w_q).reshape(B, T, XATTN_HEADS, XATTN_HEAD_DIM)
    k, v = jnp.split(m @ w_kv, 2, axis=-1)
    k = k.reshape(B, MEM_LEN, XATTN_HEADS, XATTN_HEAD_DIM)
    v = v.reshape(B, MEM_LEN, XATTN_HEADS, XATTN_HEAD_DIM)
    s = jnp.einsum('bthd,bmhd->bhtm', q, k).astype(jnp.float32) * (XATTN_HEAD_DIM ** -0.5)
    p = jax.nn.softmax(s, axis=-1)
    o = jnp.einsum('bhtm,bmhd->bthd', p, v.astype(jnp.float32)).reshape(B, T, D_MODEL)
    return o @ w_o

def setup_inputs(seed: int = 0) -> dict:
    key = jax.random.key(seed)
    ks = jax.random.split(key, 26)
    L = DEPTH
    f32 = jnp.float32
    nrm = lambda k, shape, s: jax.random.normal(k, shape, f32) * s
    return {
        "x": nrm(ks[0], (BATCH, SEQ, D_MODEL), 1.0),
        "mem": nrm(ks[1], (BATCH, MEM_LEN, D_MODEL), 1.0),
        "norm_mix": 1.0 + nrm(ks[2], (L, D_MODEL), 0.02),
        "w_in": nrm(ks[3], (L, D_MODEL, IN_WIDTH), D_MODEL ** -0.5),
        "rwkv_mu": jax.random.uniform(ks[4], (L, RWKV_IN), f32),
        "rwkv_w0": jax.random.uniform(ks[5], (L, RWKV_WIDTH), f32, -3.0, 1.0),
        "rwkv_w_up": nrm(ks[6], (L, DECAY_LORA, RWKV_WIDTH), 0.1 * DECAY_LORA ** -0.5),
        "rwkv_a0": nrm(ks[7], (L, RWKV_WIDTH), 0.1),
        "rwkv_a_up": nrm(ks[8], (L, ICLR_LORA, RWKV_WIDTH), 0.1 * ICLR_LORA ** -0.5),
        "rwkv_g_up": nrm(ks[9], (L, GATE_LORA, RWKV_WIDTH), GATE_LORA ** -0.5),
        "rwkv_k_k": 0.85 + nrm(ks[10], (L, RWKV_WIDTH), 0.02),
        "rwkv_k_a": 1.0 + nrm(ks[11], (L, RWKV_WIDTH), 0.02),
        "rwkv_r_k": nrm(ks[12], (L, RWKV_HEADS, HEAD_DIM), 0.1),
        "rwkv_ln_w": 1.0 + nrm(ks[13], (L, RWKV_WIDTH), 0.02),
        "rwkv_ln_b": nrm(ks[14], (L, RWKV_WIDTH), 0.01),
        "w_mix_out": nrm(ks[15], (L, MIX_WIDTH, D_MODEL), MIX_WIDTH ** -0.5),
        "norm_xattn": 1.0 + nrm(ks[16], (L, D_MODEL), 0.02),
        "norm_mem": 1.0 + nrm(ks[17], (L, D_MODEL), 0.02),
        "w_xq": nrm(ks[18], (L, D_MODEL, D_MODEL), D_MODEL ** -0.5),
        "w_xkv": nrm(ks[19], (L, D_MODEL, 2 * D_MODEL), D_MODEL ** -0.5),
        "w_xo": nrm(ks[20], (L, D_MODEL, D_MODEL), D_MODEL ** -0.5),
        "norm_ffn": 1.0 + nrm(ks[21], (L, D_MODEL), 0.02),
        "w_ff1": nrm(ks[22], (L, D_MODEL, D_FF), D_MODEL ** -0.5),
        "w_ff2": nrm(ks[23], (L, D_FF, D_MODEL), D_FF ** -0.5),
        "norm_final": 1.0 + nrm(ks[24], (D_MODEL,), 0.02),
    }

def reference(x, mem, norm_mix, w_in, rwkv_mu, rwkv_w0, rwkv_w_up, rwkv_a0, rwkv_a_up,
              rwkv_g_up, rwkv_k_k, rwkv_k_a, rwkv_r_k, rwkv_ln_w, rwkv_ln_b, w_mix_out,
              norm_xattn, norm_mem, w_xq, w_xkv, w_xo, norm_ffn, w_ff1, w_ff2, norm_final):
    h = x.astype(jnp.float32)
    for l in range(DEPTH):
        u = rms_norm(h, norm_mix[l])
        z = u @ w_in[l]
        y_rwkv = rwkv7_time_mix(z[..., :RWKV_IN], rwkv_mu[l], rwkv_w0[l], rwkv_w_up[l],
                                rwkv_a0[l], rwkv_a_up[l], rwkv_g_up[l], rwkv_k_k[l],
                                rwkv_k_a[l], rwkv_r_k[l], rwkv_ln_w[l], rwkv_ln_b[l])
        q, k, v = jnp.split(z[..., RWKV_IN:], 3, axis=-1)
        y_moba = moba_attention(q, k, v)
        h = h + jnp.concatenate([y_rwkv, y_moba], axis=-1) @ w_mix_out[l]
        h = h + memory_cross_attention(rms_norm(h, norm_xattn[l]), rms_norm(mem, norm_mem[l]),
                                       w_xq[l], w_xkv[l], w_xo[l])
        a = jnp.square(jax.nn.relu(rms_norm(h, norm_ffn[l]) @ w_ff1[l]))
        h = h + a @ w_ff2[l]
    return rms_norm(h, norm_final).astype(x.dtype)


_drawn_inputs = setup_inputs


def setup_inputs(seed=0):
    import zlib

    import numpy as np

    out = dict(_drawn_inputs(seed))
    spreads = {}
    factors = {'norm_mix': 3.729,
     'rwkv_w_up': 8.0,
     'rwkv_a0': 3.055,
     'rwkv_a_up': 3.557,
     'rwkv_k_k': 200.0,
     'rwkv_k_a': 6.699,
     'rwkv_ln_w': 49.143,
     'rwkv_ln_b': 172.425,
     'norm_xattn': 8.0,
     'norm_mem': 8.0,
     'norm_ffn': 16.98,
     'norm_final': 23.547}
    for name, (base, spread) in spreads.items():
        noise = np.random.default_rng([zlib.crc32(name.encode()), seed]).standard_normal(out[name].shape)
        drawn = base * np.exp(spread * noise) if base else spread * noise
        out[name] = __import__('jax').numpy.asarray(drawn.astype(out[name].dtype))
    for name, factor in factors.items():
        out[name] = (out[name] * factor).astype(out[name].dtype)
    return out
```

```python
import math
from contextlib import ExitStack

import concourse.bass as bass
from concourse import mybir

D, T, M = 1024, 256, 256
KT = D // 128
RW, NH, HD = 512, 8, 64
NP = RW // 128
CH, BLK = 32, 16
NCH = T // CH
NG = 4
DECAY = math.exp(-0.5)
GN_EPS, NORM_EPS = 64e-5, 1e-6
XH, XD = 4, 256
NF = 8
NT = T // 128
NRAW, NSPLIT = 3, 3
NEG = -1e30

PARAMS = [("norm_mix", 8), ("norm_mem", 8), ("norm_xattn", 8), ("norm_ffn", 8), ("norm_final", 8),
          ("rwkv_mu", 14), ("rwkv_w0", 4), ("rwkv_a0", 4), ("rwkv_k_k", 4), ("rwkv_k_a", 4),
          ("rwkv_r_k", 4), ("rwkv_ln_w", 4), ("rwkv_ln_b", 4)]
ROW = {}
for _n, _c in PARAMS:
    ROW[_n] = sum(c for _, c in ROW.values()), _c
NROW = sum(c for _, c in PARAMS)


def units():
    out = [("z", "w_in", 0, 256 * j, j) for j in (6, 2, 3, 0, 1, 4, 5)]
    base = 3 * RW + 256
    out += [("mq", "w_in", 0, base + 256 * j, j) for j in range(4)]
    out += [("mv", "w_in", 0, base + 2 * RW + 256 * j, j) for j in range(2)]
    out += [("xk", "w_xkv", 0, 256 * j, j) for j in range(4)]
    out += [("xv", "w_xkv", 0, D + 256 * j, j) for j in range(2)]
    out += [("mix", "w_mix_out", 0, 256 * j, j) for j in range(4)]
    out += [("xv", "w_xkv", 0, D + 256 * j, j) for j in range(2, 4)]
    out += [("xq", "w_xq", 0, 256 * j, j) for j in range(4)]
    out += [("xo", "w_xo", 0, 256 * j, j) for j in range(4)]
    for g in range(NF + 1):
        if g < NF:
            out += [("f1", "w_ff1", 0, 512 * g + 256 * j, 2 * g + j) for j in range(2)]
        if g:
            out += [("f2", "w_ff2", 4 * (g - 1), 512 * j, 2 * j) for j in range(2)]
    return out


UNITS = units()
OUTS = []
for _u, (_w, _s, _r, _c, _j) in enumerate(UNITS):
    if _w == "f2":
        OUTS += [(_u, 2 * _u + _i, 2 * _u + _i, _w, _j + _i) for _i in range(2)]
    else:
        OUTS.append((_u, 2 * _u, 2 * _u + 1, _w, _j))
OUT_OF_HALF = {_s: _o for _o, _x in enumerate(OUTS) for _s in range(_x[1], _x[2] + 1)}
FIRST = {_x[3]: _o for _o, _x in reversed(list(enumerate(OUTS)))}
LAST = {_x[3]: _o for _o, _x in enumerate(OUTS)}

QUARTERS = []
for _u in range(len(UNITS)):
    _late = {"mix": 0, "xo": 1, "f1": 1}.get(UNITS[_u][0])
    if UNITS[_u][4] == 0 and _late is not None:
        QUARTERS += [(2 * _u + _i, _late ^ _p ^ 1) for _i, _p in
                     ((0, 0), (2, 0), (0, 1), (1, 0), (1, 1), (2, 1), (3, 0), (3, 1))]
    elif UNITS[_u][4] != 1 or _late is None:
        QUARTERS += [(2 * _u + _i, _p) for _i in range(2) for _p in range(2)]
BEGUN, DONE = {}, {}
for _q, (_s, _) in enumerate(QUARTERS):
    BEGUN.setdefault(_s, _q)
    DONE[_s] = _q
ENDS = {DONE[_x[2]]: _o for _o, _x in enumerate(OUTS)}
AFTER = {_q + (0 if _o in [LAST[_w] for _w in ("xv", "xo", "f2")] else 1): _o for _q, _o in ENDS.items()}


def nth(o):
    return sum(x[3] == OUTS[o][3] for x in OUTS[:o])


def in_order(do):
    step = [0]

    def moba():
        i, part = divmod(step[0], 3)
        step[0] += 1
        if part == 0:
            if 0 < i <= NH:
                do.weigh("m", i - 1)
            if 2 <= i < NH + 2:
                do.values("m", i - 2)
        elif part == 1 and 0 < i <= NH:
            do.turn("m", i - 1)
        elif part == 2 and i < NH:
            do.scores("m", i)

    do.params(0)
    for q in range(KT // 2):
        do.load(0, q)
    do.stats(0)
    do.diagonal(0)
    do.params(1)
    do.dense(2)
    do.spread(0)
    do.dense(4)
    do.gates()
    do.dense(2)
    do.lora()
    do.dense(1)
    do.rates()
    do.dense(1)
    do.sums()
    do.dense(2)
    do.decays()
    do.dense(4)
    do.key_sums()
    do.dense(1)
    do.key_norm()
    do.stats(1)
    do.diagonal(1)
    do.dense(1)
    do.spread(1)
    do.keys(0)
    do.dense(2)
    do.keys(1)
    do.dense(2)
    do.keys(2)
    do.dense(2)
    do.keys(3)
    do.dense(3)
    do.reads()
    do.dense(3)
    do.tokens()
    do.dense(3)
    do.bonus()
    do.dense(1)
    for g in range(NG):
        for n, stage in enumerate((do.mats, do.nmat, do.pow2, do.pow4, do.pow8, do.sides, do.solve, do.carry,
                                   do.solved, do.outq)):
            stage(g)
            if g < 2:
                do.dense(2 if n == 0 else 1)
            else:
                moba()
                do.dense((1, 0, 0, 1, 0, 1, 0, 1, 0, 0)[n])
            if g == 0 and n in (2, 4, 6, 8):
                do.load(1, n // 2 - 1)
    do.phi()
    do.psi(0)
    for c in range(1, NCH - 1):
        do.psi(c)
        moba()
        do.state(c)
        do.dense(1)
    for stage, n in ((do.states_out, 1), (do.center, 1), (do.deviation, 1), (do.normalize, 1), (do.gate, 0)):
        stage()
        do.dense(n)
    while step[0] < 3 * (NH + 2):
        moba()
    do.dense(PHASE["mix"] - do.at())
    for j in range(4):
        do.dense(1)
        do.operand("mix", j)
    do.rms(2)
    do.dense(4)
    for i in range(XH + 1):
        do.dense(1)
        if i >= 2:
            do.turn("x", i - 2)
        if i:
            do.scores("x", i - 1)
        do.dense(1)
        if i:
            do.weigh("x", i - 1)
        do.dense(1 if i < XH else 0)
        if i >= 2:
            do.values("x", i - 2)
        do.dense(1 if i < XH else 0)
    do.turn("x", XH - 1)
    do.values("x", XH - 1)
    do.dense(PHASE["xo"] - do.at())
    do.dense(2)
    do.rms(3)
    do.dense(PHASE["f2"] - do.at())
    do.final_rms()
    do.finish()


PHASE = {_x[3]: 2 * (_x[2] + 1) for _x in OUTS}


class Parts:

    def __init__(self, dense, at, **parts):
        self.dense, self.at = dense, at
        skip = lambda *index: None
        self.params = parts.get("params", skip)
        self.load, self.rms = parts.get("load", skip), parts.get("rms", skip)
        self.stats, self.spread = parts.get("stats", skip), parts.get("spread", skip)
        self.diagonal, self.rates = parts.get("diagonal", skip), parts.get("rates", skip)
        self.gates, self.lora = parts.get("gates", skip), parts.get("lora", skip)
        self.sums, self.decays = parts.get("sums", skip), parts.get("decays", skip)
        self.key_sums = parts.get("key_sums", skip)
        self.key_norm, self.keys = parts.get("key_norm", skip), parts.get("keys", skip)
        self.reads, self.bonus = parts.get("reads", skip), parts.get("bonus", skip)
        self.tokens = parts.get("tokens", skip)
        self.mats, self.nmat = parts.get("mats", skip), parts.get("nmat", skip)
        self.pow2, self.pow4, self.pow8 = (parts.get(n, skip) for n in ("pow2", "pow4", "pow8"))
        self.sides, self.solve = parts.get("sides", skip), parts.get("solve", skip)
        self.carry, self.solved = parts.get("carry", skip), parts.get("solved", skip)
        self.outq, self.phi = parts.get("outq", skip), parts.get("phi", skip)
        self.psi, self.state = parts.get("psi", skip), parts.get("state", skip)
        self.states_out, self.center = parts.get("states_out", skip), parts.get("center", skip)
        self.deviation, self.normalize = parts.get("deviation", skip), parts.get("normalize", skip)
        self.operand = parts.get("operand", skip)
        self.final_rms = parts.get("final_rms", skip)
        self.gate, self.finish = parts.get("gate", skip), parts.get("finish", skip)
        self.scores, self.weigh = parts.get("scores", skip), parts.get("weigh", skip)
        self.turn, self.values = parts.get("turn", skip), parts.get("values", skip)


def build(nc, io, out):
    f32, f32r = mybir.dt.float32, mybir.dt.float32r
    ALU, ACT, AX = mybir.AluOpType, mybir.ActivationFunctionType, mybir.AxisListType
    ctx = ExitStack()
    with ctx:
        def sb(name, shape, dt=f32):
            return ctx.enter_context(nc.sbuf_tensor(name, shape, dt))

        def sem(name):
            return ctx.enter_context(nc.semaphore(name))

        def flat(x):
            return x.rearrange("p a t -> p (a t)")

        def by_token(x):
            return flat(x).rearrange("p (n c) -> p n c", n=NT)

        raw = sb("raw", [128, NRAW, 8 * 256])
        w_hi = sb("w_hi", [128, NSPLIT, 1024], f32r)
        w_lo = sb("w_lo", [128, NSPLIT, 1024], f32r)
        op_hi = [sb(f"op{i}_hi", [128, KT, T], f32r) for i in range(2)]
        op_lo = [sb(f"op{i}_lo", [128, KT, T], f32r) for i in range(2)]
        hT = sb("hT", [128, KT, T])
        rinv = sb("rinv", [128, 2, T])
        tmp = sb("tmp", [128, 2, 512])
        zT = sb("zT", [128, 14, T])
        mqk = sb("mqk", [128, 8, T])
        mval = sb("mval", [128, NT, RW])
        xkey = sb("xkey", [128, KT, M])
        xval = sb("xval", [128, NT, D])
        prob = sb("prob", [128, NT, 256])
        probT = sb("probT", [128, NT, 256])
        small = sb("small", [128, 16])
        s0 = sb("s0", [128, NP, T])
        s1 = sb("s1", [128, NP, T])
        s2 = sb("s2", [128, NP, T])
        s3 = sb("s3", [128, NP, T])
        s4 = sb("s4", [128, NP, T])
        AR = sb("AR", [128, NP, NT, 2, 128])
        btok = sb("btok", [128, NT, RW])
        U = sb("U", [128, 2 * NH, 128])
        X = sb("X", [128, 4, 512])
        neu = sb("neu", [128, 5, 4, 128])
        pend = sb("pend", [128, NP, NCH])
        par = sb("par", [128, NROW])
        onemu = sb("onemu", [128, 14])
        ident = sb("ident", [128, 128])
        ones = sb("ones", [128, 128])
        hblock = sb("hblock", [128, 128])
        maskX = sb("maskX", [128, 4, 128])
        mask_d = sb("mask_d", [128, 128])
        mask_n = sb("mask_n", [128, 128])
        causal = sb("causal", [128, NT, 256])
        ind = sb("ind", [128, NP, 8])
        indT = sb("indT", [8, NP, 128])
        eps = sb("eps", [128, 2])
        row_sum = sb("row_sum", [128, 4])
        one_k_a = sb("one_k_a", [128, NP])
        ktok, vtok = by_token(zT[:, 4:8, :]), by_token(zT[:, 0:4, :])
        prow = prob[:, 0, 0:128]
        stage = [xval, by_token(xkey[:, :, :])]
        reset = flat(X[:, :, :])[:, 0:NP * T]
        PHI = flat(X[:, :, :])[:, 0:6 * 256].rearrange("p (c h k) -> p c h k", c=6, h=NP)
        states = neu[:, :, :, :].rearrange("p a b c -> p (a b c)")[:, 0:7 * 256]\
            .rearrange("p (c h k) -> p c h k", c=7, h=NP)
        hsum = zT[0:8, 12, :]
        lora_up = flat(U[:, 0:4, :])
        gate_up = AR[:, 0, :, :, :].rearrange("p n a t -> p (n a t)")
        xqT = zT[:, 0:8, :]
        sq_out = neu[:, :, :, :].rearrange("p a b c -> p (a b c)")[:, 0:D]
        diagonal = [x.rearrange("p (n c) -> p n c", n=NT) for x in (prob[:, 1, :], probT[:, 0, :])]
        square, square_sum = s1[:, 0:2, :], s2[:, 0:2, :]
        ostage = by_token(xkey[:, :, :])

        bank = [ctx.enter_context(nc.psum_tensor(f"bank{i}", [128, 512], f32)) for i in range(8)]
        B, dense_bank = bank[0:6], bank[6:8]

        raw_in = [sem(f"raw_in{i}") for i in range(NRAW)]
        x_in, mem_in, mix_in = sem("x_in"), sem("mem_in"), sem("mix_in")
        act_sums, act_root, dve_diag, pe_spread_rms = sem("act_sums"), sem("act_root"), sem("dve_diag"), sem("pe_spread_rms")
        dve_copy, act_rest, act_factor, pool_tails = sem("dve_copy"), sem("act_rest"), sem("act_factor"), sem("pool_tails")
        params_in, lora_in, gate_in, out_done = sem("params_in"), sem("lora_in"), sem("gate_in"), sem("out_done")
        hi_done, lo_done, dense_mm, out_taken = sem("hi_done"), sem("lo_done"), sem("dense_mm"), sem("out_taken")
        pool_const, pool_link, act_link, dve_link = sem("pool_const"), sem("pool_link"), sem("act_link"), sem("dve_link")
        pe_params, dve_params = sem("pe_params"), sem("dve_params")
        pe_load, act_op, dve_op = sem("pe_load"), sem("act_op"), sem("dve_op")
        pe_square, act_square, pool_square = sem("pe_square"), sem("act_square"), sem("pool_square")
        act_rms, dve_rms = sem("act_rms"), sem("dve_rms")
        pe_vturn, act_vturn, act_hidden, dve_hidden = sem("pe_vturn"), sem("act_vturn"), sem("act_hidden"), sem("dve_hidden")
        dve_shift, act_gates, pe_lora, act_lora = sem("dve_shift"), sem("act_gates"), sem("pe_lora"), sem("act_lora")
        dve_sums, act_exp = sem("dve_sums"), sem("act_exp")
        act_kk, pe_kk, dve_kk, act_kkroot, dve_kkinv = sem("act_kk"), sem("pe_kk"), sem("dve_kk"), sem("act_kkroot"), sem("dve_kkinv")
        pe_spread, dve_kk_all, dve_A = sem("pe_spread"), sem("dve_kk_all"), sem("dve_A")
        dve_keys, dve_reads = sem("dve_keys"), sem("dve_reads")
        pe_bonus, dve_bonus = sem("pe_bonus"), sem("dve_bonus")
        pe_btok, act_btok, dve_ktok, pe_vtok, act_vtok = sem("pe_btok"), sem("act_btok"), sem("dve_ktok"), sem("pe_vtok"), sem("act_vtok")
        pe_mats, dve_mats, pe_nmat, dve_nmat = sem("pe_mats"), sem("dve_mats"), sem("pe_nmat"), sem("dve_nmat")
        pe_pow2, act_pow2, dve_pow2 = sem("pe_pow2"), sem("act_pow2"), sem("dve_pow2")
        pe_pow4, act_pow4, dve_pow4 = sem("pe_pow4"), sem("act_pow4"), sem("dve_pow4")
        pe_pow8, act_pow8, dve_pow8 = sem("pe_pow8"), sem("act_pow8"), sem("dve_pow8")
        pe_sides, act_sides, dve_inverse = sem("pe_sides"), sem("act_sides"), sem("dve_inverse")
        pe_solve, act_solve, pe_carry, act_carry = sem("pe_solve"), sem("act_solve"), sem("pe_carry"), sem("act_carry")
        pe_solved, dve_solved = sem("pe_solved"), sem("dve_solved")
        pe_outq, act_out, dve_q = sem("pe_outq"), sem("act_out"), sem("dve_q")
        pe_phi, act_phi, pe_phi_half = sem("pe_phi"), sem("act_phi"), sem("pe_phi_half")
        pe_psi, dve_psi, pe_state, dve_state = sem("pe_psi"), sem("dve_psi"), sem("pe_state"), sem("dve_state")
        pe_states_out, dve_states_out = sem("pe_states_out"), sem("dve_states_out")
        pe_mean, dve_center, act_dev = sem("pe_mean"), sem("dve_center"), sem("act_dev")
        pe_var, act_std, dve_std = sem("pe_var"), sem("act_std"), sem("dve_std")
        pe_norm, dve_norm, pe_gate, dve_gate = sem("pe_norm"), sem("dve_norm"), sem("pe_gate"), sem("dve_gate")
        pe_scores, dve_scores, act_prob, dve_prob = sem("pe_scores"), sem("dve_scores"), sem("act_prob"), sem("dve_prob")
        pe_turn, act_turn, pe_values, act_values, dve_values = (
            sem(n) for n in ("pe_turn", "act_turn", "pe_values", "act_values", "dve_values"))
        dve_gain, dve_final, pe_final, act_final = sem("dve_gain"), sem("dve_final"), sem("pe_final"), sem("act_final")

        def gain(name, k):
            return par[:, ROW[name][0] + k:ROW[name][0] + k + 1]

        def pair(x):
            return x.rearrange("p (a t) -> p a t", a=2)

        def quad(x):
            return x.rearrange("p (a t) -> p a t", a=4)

        def rows(h):
            return slice(HD * (h % 2), HD * (h % 2) + HD)

        def cols(h):
            return slice(HD * h, HD * h + HD)

        def unit_of(g, j):
            return g // 2, 4 * (g % 2) + j

        def tokens_of(n):
            return slice(128 * n, 128 * n + 128)

        def split_views(s):
            u, i = divmod(s, 2)
            k, n = (4, 256) if UNITS[u][0] == "f2" else (8, 128)
            r = raw[:, u % NRAW, :].rearrange("p (k c) -> p k c", k=k)[:, :, n * i:n * i + n]
            return r, lambda w: w[:, s % NSPLIT, :].rearrange("p (k c) -> p k c", k=k)

        def head_no(who, h):
            return h if who == "m" else NH + h

        def op_no(what, j):
            return {"x": 0, "mem": 4, "mix": 8, "xo": 12}[what] + j

        def load_bank(m, q):
            return B[q] if m == 0 else B[4 + q % 2]

        block = ctx.enter_context(nc.Block())

        @block.sync
        def _(sp):
            sp.dma_start(stage[0][:, :, :], io["x"].rearrange("b (n p) d -> p (b n) d", p=128)).then_inc(x_in, 16)
            sp.dma_start(prow[0:8, :], io["norm_mix"].rearrange("l (r p) -> (l r) p", p=128)).then_inc(mix_in, 16)

            def load_unit(u):
                what, src, r, c, _ = UNITS[u]
                if u >= NRAW:
                    sp.wait_ge(hi_done, 2 * (u - NRAW) + 2)
                    sp.wait_ge(lo_done, 2 * (u - NRAW) + 2)
                w = io[src].rearrange("l (k p) n -> p (l k) n", p=128)
                k, n = (4, 512) if what == "f2" else (8, 256)
                sp.dma_start(raw[:, u % NRAW, :].rearrange("p (k c) -> p k c", k=k),
                             w[:, r:r + k, c:c + n]).then_inc(raw_in[u % NRAW], 16)

            load_unit(0)
            for name, (r, c) in ROW.items():
                if name != "norm_mix":
                    v = io[name]
                    v = v.rearrange("l h d -> (l h d)") if len(v.shape) == 3 else \
                        v.rearrange("l d -> (l d)") if len(v.shape) == 2 else v
                    sp.dma_start(prow[r:r + c, :], v.rearrange("(r p) -> r p", p=128)).then_inc(params_in, 16)
            sp.dma_start(lora_up[0:64, :], io["rwkv_w_up"].rearrange("l r c -> (l r) c")).then_inc(lora_in, 16)
            sp.dma_start(lora_up[64:128, :], io["rwkv_a_up"].rearrange("l r c -> (l r) c")).then_inc(lora_in, 16)
            sp.dma_start(stage[1], io["mem"].rearrange("b (n p) d -> p (b n) d", p=128)).then_inc(mem_in, 16)
            for u in range(1, len(UNITS)):
                load_unit(u)
            o = out.rearrange("b (n p) d -> p (b n) d", p=128)
            for q, (done, count) in enumerate(((act_final, 1), (act_final, 2), (dve_final, 1), (dve_final, 2))):
                sp.wait_ge(done, count)
                sp.dma_start(o[:, :, 256 * q:256 * q + 256], ostage[:, :, 256 * q:256 * q + 256]).then_inc(out_done, 16)
            sp.wait_ge(out_done, 64)

        @block.gpsimd
        def _(pool):
            n = [0]

            def link(ins):
                n[0] += 1
                ins.then_inc(pool_link, 1)
                pool.wait_ge(pool_link, n[0])

            def select(ap, pattern, base, cm, op=ALU.is_ge, fill=0.0):
                link(nc.gpsimd.affine_select(out=ap, in_=ap, compare_op=op, fill=fill, base=base,
                                             pattern=pattern, channel_multiplier=cm))

            link(nc.gpsimd.memset(ident[:, :], 0.0))
            select(ident[:, :], [[-1, 128]], 0, 1, ALU.not_equal, 1.0)
            nc.gpsimd.memset(eps[:, 0:1], NORM_EPS)
            nc.gpsimd.memset(ones[:, :], 1.0 / D).then_inc(pool_const, 1)
            for t, v in ((hblock, 1.0 / HD), (maskX, 1.0), (mask_d, 1.0), (mask_n, 1.0), (ind, 1.0), (indT, 1.0),
                         (causal, 0.0)):
                nc.gpsimd.memset(t[:], v)
            nc.gpsimd.memset(reset, 1.0)
            link(nc.gpsimd.memset(eps[:, 1:2], GN_EPS))
            link(nc.gpsimd.memset(reset.rearrange("p (c t) -> p c t", t=CH)[:, :, 0:1], 0.0))
            hb = hblock[:, :].rearrange("p (b k) -> p b k", b=2)
            select(hb, [[-HD, 2], [0, HD]], 0, 1)
            select(hb, [[HD, 2], [0, HD]], HD - 1, -1)
            select(ind[:, :, :], [[128, NP], [-HD, 8]], 0, 1)
            select(ind[:, :, :], [[-128, NP], [HD, 8]], HD - 1, -1)
            it = indT[:, :, :].rearrange("j n (b k) -> j n b k", b=2)
            select(it, [[-2, NP], [-1, 2], [0, HD]], 0, 1, ALU.is_equal)
            for part in range(4):
                m = maskX[:, part, :]
                select(m, [[1, 128]], 0 if part % 2 else -1, -1)
                select(m.rearrange("p (c r) -> p c r", r=CH), [[-CH, 128 // CH], [0, CH]], 0, 1)
            for m, sign in ((mask_d, -1), (mask_n, 1)):
                select(m[:, :], [[-sign, 128]], -1, sign)
                mb = m[:, :].rearrange("p (c r) -> p c r", r=BLK)
                select(mb, [[-BLK, 128 // BLK], [0, BLK]], 0, 1)
                select(mb, [[BLK, 128 // BLK], [0, BLK]], BLK - 1, -1)
            link(nc.gpsimd.tensor_tensor(maskX[:, 0, :], maskX[:, 0, :], mask_d[:, :], ALU.subtract))
            nc.gpsimd.affine_select(out=causal[:, :, :], in_=causal[:, :, :], compare_op=ALU.is_ge, fill=NEG, base=0,
                                    pattern=[[128, NT], [-1, 256]], channel_multiplier=1).then_inc(pool_const, 1)
            pool.wait_ge(dve_keys, 1)
            at_end = pend[:, :, :].rearrange("p a c -> p (a c)").unsqueeze(2).to_broadcast([128, NP * NCH, CH])
            nc.gpsimd.tensor_tensor(s0[:, :, :].rearrange("p a (c t) -> p (a c) t", t=CH),
                                    s3[:, :, :].rearrange("p a (c t) -> p (a c) t", t=CH), at_end, ALU.mult)
            nc.gpsimd.tensor_tensor(s1[:, :, :].rearrange("p a (c t) -> p (a c) t", t=CH),
                                    s4[:, :, :].rearrange("p a (c t) -> p (a c) t", t=CH), at_end, ALU.mult)\
                .then_inc(pool_tails, 1)
            pool.wait_ge(dve_q, NG)
            pool.dma_start(gate_up, io["rwkv_g_up"].rearrange("l r c -> (l r) c")).then_inc(gate_in, 16)
            for count, what in enumerate(("mix", "xo")):
                for j in range(4):
                    pool.wait_ge(out_taken, FIRST[what] + j + 1)
                    if j == 0 and count:
                        pool.wait_ge(pe_square, 1)
                    h = hT[:, 2 * j:2 * j + 2, :]
                    if j == 0:
                        link(nc.gpsimd.tensor_tensor(square_sum, h, h, ALU.mult))
                        continue
                    link(nc.gpsimd.tensor_tensor(square, h, h, ALU.mult))
                    last = nc.gpsimd.tensor_tensor(square_sum, square_sum, square, ALU.add)
                    if j < 3:
                        link(last)
                last.then_inc(pool_square, 1)

        @block.tensor
        def _(pe):
            mm, turn_op = nc.tensor.matmul, nc.tensor.transpose
            pe.wait_ge(pool_const, 1)
            at = [0]

            def quarter(q):
                s, part = QUARTERS[q]
                what, _, r, _, _ = UNITS[s // 2]
                o = OUT_OF_HALF[s]
                deep = what == "f2"
                if q == BEGUN[s]:
                    if s == OUTS[o][1] and o >= 2:
                        pe.wait_ge(out_taken, o - 1)
                    pe.wait_ge(hi_done, s + 1)
                    pe.wait_ge(lo_done, s + 1)
                which = 1 if what in ("xk", "xv", "xo", "f2") else 0
                opening = o - FIRST[what] <= (what in ("xo", "f1")) and s == OUTS[o][1] and not deep
                if what == "mix" and q == BEGUN[s] and s == OUTS[FIRST[what]][1]:
                    pe.wait_ge(dve_values, NH)
                if what == "mix" and s == OUTS[FIRST[what]][1] and part == 0:
                    pe.wait_ge(dve_gate, 2)
                if deep and s % 4 == 0 and q == BEGUN[s]:
                    pe.wait_ge(dve_hidden, 2 * (r // 4) + 2)
                b = dense_bank[o % 2]
                _, view = split_views(s)
                wh, wl = view(w_hi), view(w_lo)
                if deep:
                    todo = [(k, 4 * (r // 4 % 2) + k, 128 * part, part * T, k == 0, k == 3) for k in range(4)]
                else:
                    todo = [(k, k, 0, (s % 2) * T, q == BEGUN[s] and k % 4 == 0, q == DONE[s] and k % 4 == 3)
                            for k in range(4 * part, 4 * part + 4)]
                for k, xk, c, t, first, final in todo:
                    if opening and what == "xo" and k % 2 == 0:
                        pe.wait_ge(dve_values, NH + k // 2 + 1)
                    if opening and what in ("z", "xk", "xq", "f1") and k % 2 == 0:
                        pe.wait_ge(dve_op, op_no({"z": "x", "xk": "mem", "xq": "mix", "f1": "xo"}[what], k // 2) + 1)
                    dst = b[:, t:t + T]
                    mm(dst, wh[:, k, c:c + 128], op_hi[which][:, xk, :], start=first, stop=False)
                    mm(dst, wh[:, k, c:c + 128], op_lo[which][:, xk, :], start=False, stop=False)
                    last = mm(dst, wl[:, k, c:c + 128], op_hi[which][:, xk, :], start=False, stop=final)
                if q == DONE[s]:
                    last.then_inc(dense_mm, 1)
                if q in AFTER:
                    follow(AFTER[q])

            def follow(o):
                if OUTS[o][3] in ("mv", "xv"):
                    vturn(o)
                if OUTS[o][3] == "f2" and o >= len(OUTS) - 4:
                    squares(o - len(OUTS) + 4)
                    turn_out(o - len(OUTS) + 4)

            def dense(n):
                for q in range(at[0], at[0] + n):
                    quarter(q)
                at[0] += n

            bank5 = [None]

            def vturn(o):
                pe.wait_ge(out_taken, o + 1)
                if bank5[0]:
                    pe.wait_ge(*bank5[0])
                for n in range(NT):
                    for a in range(2):
                        last = turn_op(B[5][:, 256 * n + 128 * a:256 * n + 128 * a + 128],
                                       tmp[:, 0, 256 * a + 128 * n:256 * a + 128 * n + 128], ident[:, :])
                last.then_inc(pe_vturn, 1)
                v = nth(o) + (2 if OUTS[o][3] == "xv" else 0)
                bank5[0] = act_vturn, v + 1

            def squares(j):
                pe.wait_ge(act_square, j + 1)
                if j == 0:
                    pe.wait_ge(act_rms, 2)
                for n in range(NT):
                    for a in range(2):
                        last = mm(B[4 + n][:, 0:1], tmp[:, 1, a * T + 128 * n:a * T + 128 * n + 128], ones[:, 0:1],
                                  start=(j == 0 and a == 0), stop=(j == 3 and a == 1))
                last.then_inc(pe_square, 1)

            def turn_out(j):
                pe.wait_ge(dve_gain, j + 1)
                for n in range(NT):
                    for a in range(2):
                        last = turn_op(B[j][:, 256 * n + 128 * a:256 * n + 128 * a + 128],
                                       zT[:, 2 * j + a, tokens_of(n)], ident[:, :])
                last.then_inc(pe_final, 1)

            def params(part):
                if part == 0:
                    pe.wait_ge(mix_in, 16)
                    turn_op(B[4][:, 0:8], prow[0:8, :], ident[0:8, 0:8]).then_inc(pe_params, 1)
                else:
                    pe.wait_ge(params_in, 16 * (len(PARAMS) - 1))
                    pe.wait_ge(dve_params, 1)
                    turn_op(B[4][:, 0:NROW], prow[0:NROW, :], ident[0:NROW, 0:NROW]).then_inc(pe_params, 1)

            def load(m, q):
                if m == 0:
                    pe.wait_ge(x_in, 16)
                elif q == 0:
                    pe.wait_ge(mem_in, 16)
                b = load_bank(m, q)
                if m and q == 0:
                    pe.wait_ge(dve_params, 2)
                    pe.wait_ge(dve_rms, 2)
                if m and q >= 2:
                    pe.wait_ge(dve_op, 4 + q - 1)
                for a in range(2):
                    for n in range(NT):
                        last = turn_op(b[:, 256 * a + 128 * n:256 * a + 128 * n + 128],
                                       stage[m][:, n, 256 * q + 128 * a:256 * q + 128 * a + 128], ident[:, :])
                last.then_inc(pe_load, 1)
                if (m, q) == (1, 3):
                    bank5[0] = dve_op, 8

            def spread(m):
                pe.wait_ge(dve_diag, m + 1)
                if m:
                    pe.wait_ge(dve_rms, 1)
                for n in range(NT):
                    last = mm(B[5][:, tokens_of(n)], ones[:, :], diagonal[m][:, n, :], start=True, stop=True)
                last.then_inc(pe_spread_rms, 1)
                bank5[0] = dve_rms, m + 1

            def rms(i):
                if i in (2, 3):
                    pe.wait_ge(pool_square, i - 1)
                    if bank5[0]:
                        pe.wait_ge(*bank5[0])
                    for a in range(2):
                        last = mm(B[5][:, 0:T], ones[:, :], square_sum[:, a, :], start=(a == 0), stop=(a == 1))
                    last.then_inc(pe_square, 1)
                bank5[0] = act_rms, i - 1

            def lora():
                pe.wait_ge(lora_in, 32)
                pe.wait_ge(act_gates, 1)
                pe.wait_ge(dve_op, 4)
                for lo in (0, 64):
                    for p in range(NP):
                        last = mm(B[lo // 32 + p // 2][:, (p % 2) * T:(p % 2) * T + T],
                                  lora_up[lo:lo + 64, tokens_of(p)], zT[lo:lo + 64, 12, :], start=True, stop=True)
                last.then_inc(pe_lora, 1)

            def head_sums(src, signal):
                for p in range(NP):
                    last = mm(B[0][0:8, 0:T], ind[:, p, :], src[:, p, :], start=(p == 0), stop=(p == NP - 1))
                last.then_inc(signal, 1)

            def by_pair(banks, lhs, rhs, signal):
                for p in range(NP):
                    last = mm(B[banks[p // 2]][:, (p % 2) * T:(p % 2) * T + T], lhs(p), rhs(p), start=True, stop=True)
                last.then_inc(signal, 1)

            def key_sums():
                pe.wait_ge(pool_const, 2)
                pe.wait_ge(act_kk, 1)
                pe.wait_ge(act_lora, 1)
                head_sums(s4, pe_kk)

            def keys(step):
                if step:
                    return
                pe.wait_ge(dve_kkinv, 1)
                by_pair((1, 2), lambda p: indT[:, p, :], lambda p: hsum[:, :], pe_spread)

            def tokens():
                pe.wait_ge(pool_tails, 1)
                pe.wait_ge(dve_kk_all, 1)
                for src, b in ((s0, 0), (s1, 2)):
                    for n in range(NT):
                        for p in range(NP):
                            last = turn_op(B[b + n][:, tokens_of(p)], src[:, p, tokens_of(n)], ident[:, :])
                last.then_inc(pe_btok, 1)

            def bonus():
                pe.wait_ge(dve_shift, 7)
                pe.wait_ge(act_btok, 1)
                pe.wait_ge(dve_ktok, 1)
                for n in range(NT):
                    for p in range(NP):
                        last = turn_op(B[1 + n][:, tokens_of(p)], zT[:, 8 + p, tokens_of(n)], ident[:, :])
                last.then_inc(pe_vtok, 1)
                pe.wait_ge(dve_reads, 1)
                by_pair((3, 0), lambda p: hblock[:, :], lambda p: s2[:, p, :], pe_bonus)

            def mats(g):
                if g == 0:
                    pe.wait_ge(act_vtok, 1)
                    pe.wait_ge(dve_bonus, 1)
                else:
                    pe.wait_ge(act_out, g)
                    pe.wait_ge(dve_q, g)
                for j in range(4):
                    n, h = unit_of(g, j)
                    both = AR[rows(h), h // 2, n, :, :].rearrange("p a t -> p (a t)")
                    mm(B[j][:, 0:256], s3[rows(h), h // 2, tokens_of(n)], both, start=True, stop=True)
                    last = mm(B[j][:, 256:512], s4[rows(h), h // 2, tokens_of(n)], both, start=True, stop=True)
                last.then_inc(pe_mats, 1)

            def nmat(g):
                pe.wait_ge(dve_mats, g + 1)
                for j in range(4):
                    n, h = unit_of(g, j)
                    last = mm(B[j % 2][:, tokens_of(j // 2)], AR[rows(h), h // 2, n, 0, :],
                              s3[rows(h), h // 2, tokens_of(n)], start=True, stop=True)
                last.then_inc(pe_nmat, 1)

            def four(b, lhs, rhs):
                for j in range(4):
                    last = mm(B[b][:, tokens_of(j)], neu[:, lhs, j, :], neu[:, rhs, j, :], start=True, stop=True)
                return last

            def pow2(g):
                pe.wait_ge(dve_nmat, g + 1)
                four(2, 1, 0)
                four(3, 0, 1).then_inc(pe_pow2, 1)

            def pow4(g):
                pe.wait_ge(act_pow2, g + 1)
                pe.wait_ge(dve_pow2, g + 1)
                four(0, 3, 2)
                four(1, 2, 3)
                four(2, 3, 4).then_inc(pe_pow4, 1)

            def pow8(g):
                pe.wait_ge(act_pow4, g + 1)
                pe.wait_ge(dve_pow4, g + 1)
                four(3, 0, 1)
                four(0, 1, 4).then_inc(pe_pow8, 1)

            def sides(g):
                w = B[2][:, :].rearrange("p (j x k) -> p j x k", j=4, x=2)
                for j in range(4):
                    n, h = unit_of(g, j)
                    mm(w[:, j, 0, :], X[:, j, 256:384], vtok[:, n, cols(h)], start=True, stop=True)
                for j in (0, 2):
                    n, h = unit_of(g, j)
                    turn_op(w[:, j:j + 2, 1, :], AR[:, h // 2, n, 0, :], ident[:, :])
                pe.wait_ge(act_pow8, g + 1)
                pe.wait_ge(dve_pow8, g + 1)
                four(1, 2, 4).then_inc(pe_sides, 1)

            def solve(g):
                pe.wait_ge(act_sides, g + 1)
                pe.wait_ge(dve_inverse, g + 1)
                four(3, 4, 3).then_inc(pe_solve, 1)

            def carry(g):
                pe.wait_ge(act_solve, g + 1)
                for j in range(4):
                    last = mm(B[0][:, tokens_of(j)], X[:, j, 0:128], neu[:, 0, j, :], start=True, stop=True)
                last.then_inc(pe_carry, 1)

            def solved(g):
                pe.wait_ge(act_carry, g + 1)
                four(1, 4, 1).then_inc(pe_solved, 1)

            def outq(g):
                pe.wait_ge(act_solve, g + 1)
                for j in range(4):
                    n, h = unit_of(g, j)
                    mm(B[2][rows(h), tokens_of(j // 2)], vtok[:, n, cols(h)], X[:, j, 384:512], start=True, stop=False)
                    if j == 0:
                        pe.wait_ge(dve_solved, g + 1)
                    mm(B[2][rows(h), tokens_of(j // 2)], U[:, 4 * g + j, 0:HD], X[:, j, 128:256], start=False, stop=True)
                for j in range(4):
                    last = mm(B[3][rows(j), tokens_of(j // 2)], U[:, 4 * g + j, HD:128], X[:, j, 128:256],
                              start=True, stop=True)
                last.then_inc(pe_outq, 1)

            def phi():
                pe.wait_ge(act_out, NG)
                for c in range(1, NCH - 1):
                    r = slice(CH * (c % 4), CH * (c % 4) + CH)
                    for h in range(NH):
                        o = 256 * ((c - 1) // 3) + 64 * (h // 2)
                        last = mm(B[(c - 1) % 3][rows(h), o:o + 64], U[r, NH * (c // 4) + h, HD:128],
                                  btok[r, c // 4, cols(h)], start=True, stop=True)
                    if c == 3:
                        last.then_inc(pe_phi_half, 1)
                        pe.wait_ge(pe_phi_half, 1)
                last.then_inc(pe_phi, 1)

            def psi(c):
                if c == 0:
                    pe.wait_ge(dve_q, NG)
                elif c == 1:
                    pe.wait_ge(act_phi, 1)
                else:
                    pe.wait_ge(dve_psi, c - 1)
                r = slice(CH * (c % 4), CH * (c % 4) + CH)
                for h in range(NH):
                    dst = B[3 - c % 2][rows(h), 64 * (h // 2):64 * (h // 2) + 64]
                    mm(dst, btok[r, c // 4, cols(h)], U[r, NH * (c // 4) + h, 0:HD], start=True, stop=False)
                    last = mm(dst, ktok[r, c // 4, cols(h)], vtok[r, c // 4, cols(h)], start=False, stop=True)
                last.then_inc(pe_psi, 1)

            def state(c):
                pe.wait_ge(act_phi, 1)
                if c == 1:
                    pe.wait_ge(dve_psi, 1)
                else:
                    pe.wait_ge(dve_state, c - 1)
                for h in range(NH):
                    last = mm(B[c % 2][rows(h), 64 * (h // 2):64 * (h // 2) + 64], PHI[rows(h), c - 1, h // 2, :],
                              states[rows(h), c - 1, h // 2, :], start=True, stop=True)
                last.then_inc(pe_state, 1)

            def states_out():
                pe.wait_ge(dve_state, NCH - 2)
                for h in range(NH):
                    for c in range(1, NCH):
                        o = T * ((h // 2) % 2) + CH * c
                        last = mm(B[h // 4][rows(h), o:o + CH], states[rows(h), c - 1, h // 2, :],
                                  s1[rows(h), h // 2, CH * c:CH * c + CH], start=True, stop=True)
                last.then_inc(pe_states_out, 1)

            def center():
                pe.wait_ge(dve_states_out, 1)
                by_pair((2, 3), lambda p: hblock[:, :], lambda p: s0[:, p, :], pe_mean)

            def deviation():
                pe.wait_ge(act_dev, 1)
                head_sums(s1, pe_var)

            def normalize():
                pe.wait_ge(dve_std, 1)
                by_pair((1, 2), lambda p: indT[:, p, :], lambda p: hsum[:, :], pe_norm)

            def gate():
                pe.wait_ge(gate_in, 16)
                by_pair((0, 3), lambda p: gate_up[:, tokens_of(p)], lambda p: zT[:, 13, :], pe_gate)

            def scores(who, h):
                if who == "x":
                    pe.wait_ge(out_taken, FIRST["xq"] + h + 1)
                elif h == 0:
                    pe.wait_ge(out_taken, FIRST["mq"] + 4)
                no = head_no(who, h)
                if no:
                    pe.wait_ge(dve_scores, no)
                if no >= 2:
                    pe.wait_ge(act_values, no - 1)
                    pe.wait_ge(dve_values, no - 1)
                for n in range(NT):
                    dst = B[4][:, 256 * n:256 * n + 256]
                    if who == "m":
                        last = mm(dst, mqk[rows(h), h // 2, tokens_of(n)], mqk[rows(h), 4 + h // 2, :],
                                  start=True, stop=True)
                        continue
                    for a in range(2):
                        last = mm(dst, xqT[:, 2 * h + a, tokens_of(n)], xkey[:, 2 * h + a, :],
                                  start=(a == 0), stop=(a == 1))
                last.then_inc(pe_scores, 1)

            def turn(who, h):
                no = head_no(who, h)
                pe.wait_ge(dve_prob, no + 1)
                pe.wait_ge(*bank5[0])
                for k in range(2):
                    for n in range(NT):
                        last = turn_op(B[5][:, 256 * k + 128 * n:256 * k + 128 * n + 128],
                                       prob[:, n, tokens_of(k)], ident[:, :])
                last.then_inc(pe_turn, 1)
                bank5[0] = act_turn, no + 1

            def values(who, h):
                no = head_no(who, h)
                pe.wait_ge(act_turn, no + 1)
                pe.wait_ge(dve_scores, min(no + 2, NH if who == "m" else NH + XH))
                if no:
                    pe.wait_ge(dve_values, no)
                if who == "m":
                    if h == 0:
                        pe.wait_ge(act_vturn, 2)
                    mm(B[4][rows(h), 0:256], mval[:, 0, cols(h)], probT[:, 0, :], start=True, stop=False)
                    last = mm(B[4][rows(h), 128:256], mval[:, 1, cols(h)], probT[:, 1, 128:256], start=False, stop=True)
                else:
                    pe.wait_ge(act_vturn, 2 + h + 1)
                    for a in range(2):
                        for k in range(2):
                            c = XD * h + 128 * a
                            last = mm(B[4][:, 256 * a:256 * a + 256], xval[:, k, c:c + 128], probT[:, k, :],
                                      start=(k == 0), stop=(k == 1))
                last.then_inc(pe_values, 1)

            in_order(Parts(dense, lambda: at[0], params=params, load=load, rms=rms, spread=spread, lora=lora, key_sums=key_sums,
                           keys=keys, bonus=bonus, tokens=tokens, mats=mats, nmat=nmat, pow2=pow2, pow4=pow4,
                           pow8=pow8, sides=sides, solve=solve, carry=carry, solved=solved, outq=outq, phi=phi,
                           psi=psi, state=state, states_out=states_out, center=center, deviation=deviation,
                           normalize=normalize, gate=gate, scores=scores, turn=turn, values=values))

        @block.scalar
        def _(act):
            op = nc.scalar.activation
            act.wait_ge(pool_const, 1)
            at, links = [0], [0]

            def link(ins):
                links[0] += 1
                ins.then_inc(act_link, 1)
                act.wait_ge(act_link, links[0])

            def split_hi(s):
                u = s // 2
                act.wait_ge(raw_in[u % NRAW], 16 * (u // NRAW + 1))
                if s >= NSPLIT:
                    act.wait_ge(dense_mm, s - NSPLIT + 1)
                r, view = split_views(s)
                op(view(w_hi), r, ACT.Copy).then_inc(hi_done, 1)

            def quarter(q):
                if q % 2 == 0 and q // 2 + 2 < 2 * len(UNITS):
                    split_hi(q // 2 + 2)
                if q in AFTER:
                    follow(AFTER[q])

            def follow(o):
                what, j = OUTS[o][3:5]
                if what == "z":
                    act.wait_ge(dve_params, 2)
                    act.wait_ge(out_taken, o + 1)
                    for a in range(2):
                        t = 2 * j + a
                        last = op(zT[:, t, :], tmp[:, 0, a * T:a * T + T], ACT.Copy, scale=onemu[:, t:t + 1])
                    last.then_inc(act_rest, 1)
                if what in ("mv", "xv"):
                    vturn(o)
                if what == "xo":
                    operand(what, j)
                if what == "f1":
                    hidden(o)
                if what == "f2" and o >= len(OUTS) - 4:
                    final_square(o)

            def dense(n):
                for q in range(at[0], at[0] + n):
                    quarter(q)
                at[0] += n

            def operand(what, j):
                act.wait_ge(out_taken, FIRST[what] + j + 1)
                if what == "mix":
                    act.wait_ge(dense_mm, OUTS[LAST["mix"]][2] + 1)
                name = {"mix": "norm_xattn", "xo": "norm_ffn"}[what]
                for a in range(2):
                    last = op(op_hi[0][:, 2 * j + a, :], hT[:, 2 * j + a, :], ACT.Copy, scale=gain(name, 2 * j + a))
                last.then_inc(act_op, 1)

            def final_square(o):
                n = o - len(OUTS) + 4
                act.wait_ge(out_taken, o + 1)
                if n:
                    act.wait_ge(pe_square, 2 + n)
                else:
                    act.wait_ge(dve_hidden, 2 * NF)
                j = OUTS[o][4]
                op(pair(tmp[:, 1, :]), hT[:, 2 * j:2 * j + 2, :], ACT.Square).then_inc(act_square, 1)

            def vturn(o):
                v = nth(o) + (2 if OUTS[o][3] == "xv" else 0)
                act.wait_ge(pe_vturn, v + 1)
                dst, j = (mval if OUTS[o][3] == "mv" else xval), OUTS[o][4]
                op(dst[:, :, 256 * j:256 * j + 256], pair(B[5][:, :]), ACT.Copy).then_inc(act_vturn, 1)

            def hidden(o):
                n = nth(o)
                act.wait_ge(out_taken, o + 1)
                if n:
                    act.wait_ge(dve_hidden, n)
                k = 4 * (n // 2 % 2) + 2 * (n % 2)
                t = pair(tmp[:, 1, :])
                link(op(t, pair(tmp[:, 0, :]), ACT.Relu))
                link(op(t, t, ACT.Square))
                op(op_hi[1][:, k:k + 2, :], t, ACT.Copy).then_inc(act_hidden, 1)

            def load(m, q):
                n = 4 * m + q
                if m == 0:
                    act.wait_ge(dve_copy, q + 1)
                    if q == 0:
                        act.wait_ge(dve_params, 1)
                else:
                    act.wait_ge(pe_load, n + 1)
                src = hT[:, 2 * q:2 * q + 2, :] if m == 0 else pair(load_bank(m, q)[:, :])
                for a in range(2):
                    last = op(op_hi[m][:, 2 * q + a, :], src[:, a, :], ACT.Copy,
                              scale=gain(("norm_mix", "norm_mem")[m], 2 * q + a))
                last.then_inc(act_op, 1)
                if m == 0 and q % 2:
                    split_hi(q // 2)

            def stats(m):
                if m == 0:
                    act.wait_ge(x_in, 16)
                else:
                    act.wait_ge(mem_in, 16)
                    act.wait_ge(act_sums, 1)
                for n in range(NT):
                    last = op(sq_out, stage[m][:, n, :], ACT.Square, accum_out=row_sum[:, 2 * m + n:2 * m + n + 1])
                    if n == 0:
                        link(last)
                last.then_inc(act_sums, 1)
                act.wait_ge(act_sums, m + 1)
                r = row_sum[:, 2 * m:2 * m + 2]
                op(r, r, ACT.Sqrt, scale=1.0 / D, bias=eps[:, 0:1]).then_inc(act_root, 1)

            def rms(i):
                act.wait_ge(pe_square, i - 1)
                act.wait_ge(out_taken, FIRST[{2: "mix", 3: "xo"}[i]] + 4)
                op(rinv[:, 0, :], B[5][:, 0:T], ACT.Sqrt, bias=eps[:, 0:1]).then_inc(act_rms, 1)

            def gates():
                act.wait_ge(dve_shift, 1)
                op(zT[:, 13, :], zT[:, 13, :], ACT.Sigmoid)
                op(zT[0:64, 12, :], zT[0:64, 12, :], ACT.Tanh).then_inc(act_gates, 1)

            def rates():
                act.wait_ge(pe_lora, 1)
                for dst, b, name in ((s0, 0, "rwkv_w0"), (s3, 2, "rwkv_a0")):
                    for p in range(NP):
                        last = op(dst[:, p, :], B[b + p // 2][:, (p % 2) * T:(p % 2) * T + T], ACT.Sigmoid,
                                  bias=gain(name, p))
                last.then_inc(act_lora, 1)

            def decays():
                act.wait_ge(dve_sums, 1)
                op(s2[:, :, :], s1[:, :, :], ACT.Exp, scale=-DECAY)
                op(s0[:, :, :], s0[:, :, :], ACT.Exp, scale=-DECAY)
                op(s1[:, :, :], s1[:, :, :], ACT.Exp, scale=DECAY).then_inc(act_exp, 1)

            def key_sums():
                act.wait_ge(dve_shift, 3)
                for p in range(NP):
                    last = op(s4[:, p, :], zT[:, 4 + p, :], ACT.Square, scale=gain("rwkv_k_k", p))
                last.then_inc(act_kk, 1)

            def key_norm():
                act.wait_ge(dve_kk, 1)
                op(hsum[:, :], hsum[:, :], ACT.Sqrt).then_inc(act_kkroot, 1)

            def keys(step):
                if step == 1:
                    act.wait_ge(dve_A, 1)
                    for p in range(NP):
                        last = op(s0[:, p, :], s3[:, p, :], ACT.Identity, scale=gain("rwkv_k_a", p), bias=one_k_a[:, p:p + 1])
                    last.then_inc(act_factor, 1)

            def tokens():
                act.wait_ge(pe_btok, 1)
                op(btok[:, 0, :], B[0][:, :], ACT.Copy)
                op(btok[:, 1, :], B[1][:, :], ACT.Copy).then_inc(act_btok, 1)

            def bonus():
                act.wait_ge(pe_vtok, 1)
                act.wait_ge(dve_reads, 1)
                op(vtok[:, 0, :], B[1][:, :], ACT.Copy)
                op(vtok[:, 1, :], B[2][:, :], ACT.Copy).then_inc(act_vtok, 1)

            def pow2(g):
                act.wait_ge(pe_pow2, g + 1)
                op(neu[:, 2, :, :], quad(B[2][:, :]), ACT.Copy).then_inc(act_pow2, 1)

            def pow4(g):
                act.wait_ge(pe_pow4, g + 1)
                op(neu[:, 0, :, :], quad(B[0][:, :]), ACT.Copy)
                op(neu[:, 1, :, :], quad(B[1][:, :]), ACT.Copy).then_inc(act_pow4, 1)

            def pow8(g):
                act.wait_ge(pe_pow8, g + 1)
                op(neu[:, 2, :, :], quad(B[3][:, :]), ACT.Copy).then_inc(act_pow8, 1)

            def sides(g):
                act.wait_ge(pe_sides, g + 1)
                op(neu[:, 3, :, :], quad(B[2][:, :]), ACT.Copy).then_inc(act_sides, 1)

            def solve(g):
                act.wait_ge(pe_solve, g + 1)
                op(neu[:, 0, :, :], quad(B[3][:, :]), ACT.Copy).then_inc(act_solve, 1)

            def carry(g):
                act.wait_ge(pe_carry, g + 1)
                op(neu[:, 1, :, :], quad(B[0][:, :]), ACT.Copy).then_inc(act_carry, 1)

            def outq(g):
                act.wait_ge(pe_outq, g + 1)
                n, p = g // 2, 2 * (g % 2)
                op(s0[:, p:p + 2, tokens_of(n)], pair(B[2][:, 0:256]), ACT.Copy).then_inc(act_out, 1)

            def phi():
                act.wait_ge(pe_phi, 1)
                for b in range(3):
                    for c in range(2):
                        last = op(PHI[:, 3 * c + b, :, :].rearrange("p h k -> p (h k)"),
                                  B[b][:, 256 * c:256 * c + 256], ACT.Copy)
                last.then_inc(act_phi, 1)

            def deviation():
                act.wait_ge(dve_center, 1)
                op(s1[:, :, :], s0[:, :, :], ACT.Square).then_inc(act_dev, 1)
                act.wait_ge(pe_var, 1)
                op(hsum[:, :], B[0][0:8, 0:T], ACT.Sqrt, scale=1.0 / HD, bias=eps[0:8, 1:2]).then_inc(act_std, 1)

            def gate():
                act.wait_ge(dve_gate, 1)
                op(op_hi[0][:, 0:4, :], s0[:, :, :], ACT.Copy).then_inc(act_op, 1)

            def scores(who, h):
                act.wait_ge(dve_scores, head_no(who, h) + 1)
                for n in range(NT):
                    last = op(prob[:, n, :], prob[:, n, :], ACT.Exp, bias=small[:, n:n + 1],
                              accum_out=small[:, 2 + n:3 + n])
                last.then_inc(act_prob, 1)

            def turn(who, h):
                act.wait_ge(pe_turn, head_no(who, h) + 1)
                op(probT[:, :, :], pair(B[5][:, :]), ACT.Copy).then_inc(act_turn, 1)

            def values(who, h):
                act.wait_ge(pe_values, head_no(who, h) + 1)
                if who == "m":
                    dst, src = op_hi[0][rows(h), 4 + h // 2, :], B[4][rows(h), 0:T]
                else:
                    dst, src = op_hi[1][:, 2 * h:2 * h + 2, :], pair(B[4][:, :])
                op(dst, src, ACT.Copy).then_inc(act_values, 1)

            def final_rms():
                act.wait_ge(pe_square, 6)
                for n in range(NT):
                    last = op(row_sum[:, n:n + 1], B[4 + n][:, 0:1], ACT.Sqrt, bias=eps[:, 0:1])
                last.then_inc(act_root, 1)

            def finish():
                act.wait_ge(dve_rms, 5)
                act.wait_ge(pe_final, 4)
                for q in range(2):
                    for n in range(NT):
                        last = op(ostage[:, n, 256 * q:256 * q + 256], B[q][:, 256 * n:256 * n + 256], ACT.Copy,
                                  scale=row_sum[:, n:n + 1])
                    last.then_inc(act_final, 1)

            in_order(Parts(dense, lambda: at[0], load=load, stats=stats, rms=rms, gates=gates, rates=rates, operand=operand,
                           decays=decays, key_sums=key_sums, key_norm=key_norm, keys=keys, bonus=bonus,
                           tokens=tokens, pow2=pow2, pow4=pow4, pow8=pow8, sides=sides, solve=solve, carry=carry,
                           outq=outq, phi=phi, deviation=deviation, gate=gate, scores=scores, turn=turn,
                           values=values, final_rms=final_rms, finish=finish))

        @block.vector
        def _(dve):
            tt, ts, stt, cp = (nc.vector.tensor_tensor, nc.vector.tensor_scalar,
                               nc.vector.scalar_tensor_tensor, nc.vector.tensor_copy)
            dve.wait_ge(pool_const, 1)
            at, links = [0], [0]

            def link(ins):
                links[0] += 1
                ins.then_inc(dve_link, 1)
                dve.wait_ge(dve_link, links[0])

            def split_lo(s):
                dve.wait_ge(hi_done, s + 1)
                r, view = split_views(s)
                tt(view(w_lo), r, view(w_hi).bitcast(f32), ALU.subtract).then_inc(lo_done, 1)

            def quarter(q):
                if q % 2 == 0 and q // 2 + 2 < 2 * len(UNITS):
                    split_lo(q // 2 + 2)
                if q in AFTER and q not in ENDS:
                    follow(AFTER[q])
                if q in ENDS:
                    take(ENDS[q], *OUTS[ENDS[q]][3:5])
                    if AFTER.get(q) == ENDS[q]:
                        follow(ENDS[q])

            def follow(o):
                what, j = OUTS[o][3:5]
                if what == "z":
                    shift(nth(o), j)
                if what == "xo":
                    operand(what, j)
                if what == "f1":
                    hidden(nth(o))
                if what == "f2" and o >= len(OUTS) - 4:
                    final_gain(o, j)

            def dense(n):
                for q in range(at[0], at[0] + n):
                    quarter(q)
                at[0] += n

            def take(o, what, j):
                dve.wait_ge(dense_mm, OUTS[o][2] + 1)
                src = pair(dense_bank[o % 2][:, :])
                if what in ("mix", "xo", "f2"):
                    h = hT[:, 2 * j:2 * j + 2, :]
                    if what == "xo":
                        dve.wait_ge(pool_square, 1)
                    if what == "f2" and o < FIRST["f2"] + 4:
                        dve.wait_ge(pool_square, 2)
                    dve.wait_ge(out_taken, o)
                    tt(h, src, h, ALU.add).then_inc(out_taken, 1)
                    return
                n = nth(o)
                if what == "z" and n:
                    dve.wait_ge(dve_shift, n)
                if what in ("mv", "xv"):
                    v = n + (2 if what == "xv" else 0)
                    if v == 0:
                        dve.wait_ge(dve_shift, 7)
                    if v:
                        dve.wait_ge(pe_vturn, v)
                if what == "f1":
                    if n:
                        dve.wait_ge(act_hidden, n)
                if what in ("z", "xk", "xv"):
                    dve.wait_ge(dve_rms, 2 if what in ("xk", "xv") else 1)
                if o == FIRST["xq"]:
                    dve.wait_ge(dve_rms, 3)
                    dve.wait_ge(act_values, NH)
                if o == FIRST["f1"]:
                    dve.wait_ge(dve_rms, 4)
                dst = {"mq": mqk, "xk": xkey, "xq": xqT}.get(what)
                dst = pair(tmp[:, 0, :]) if dst is None else dst[:, 2 * j:2 * j + 2, :]
                r = 1 if what in ("xk", "xv") else 0
                tt(dst, src, rinv[:, r:r + 1, :].to_broadcast([128, 2, T]), ALU.mult).then_inc(out_taken, 1)

            def shift(n, j):
                dve.wait_ge(act_rest, n + 1)
                for a in range(2):
                    t = 2 * j + a
                    last = stt(out=zT[:, t, 1:T], in0=tmp[:, 0, a * T:a * T + T - 1], scalar=gain("rwkv_mu", t),
                               in1=zT[:, t, 1:T], op0=ALU.mult, op1=ALU.add)
                last.then_inc(dve_shift, 1)

            def operand(what, j):
                n = op_no(what, j) + (1 if what in ("mix", "xo") else 0)
                dve.wait_ge(act_op, n + 1)
                name = {"mix": "norm_xattn", "xo": "norm_ffn"}[what]
                for a in range(2):
                    k = 2 * j + a
                    last = stt(out=op_lo[0][:, k, :], in0=hT[:, k, :], scalar=gain(name, k),
                               in1=op_hi[0][:, k, :].bitcast(f32), op0=ALU.mult, op1=ALU.subtract)
                last.then_inc(dve_op, 1)

            def final_gain(o, j):
                dve.wait_ge(out_taken, o + 1)
                for k in (2 * j, 2 * j + 1):
                    last = ts(zT[:, k, :], hT[:, k, :], gain("norm_final", k), None, ALU.mult)
                last.then_inc(dve_gain, 1)

            def hidden(n):
                dve.wait_ge(act_hidden, n + 1)
                k = 4 * (n // 2 % 2) + 2 * (n % 2)
                tt(op_lo[1][:, k:k + 2, :], pair(tmp[:, 1, :]), op_hi[1][:, k:k + 2, :].bitcast(f32),
                   ALU.subtract).then_inc(dve_hidden, 1)

            def params(part):
                dve.wait_ge(pe_params, part + 1)
                if part == 0:
                    cp(par[:, 0:8], B[4][:, 0:8]).then_inc(dve_params, 1)
                    return
                link(cp(par[:, 8:NROW], B[4][:, 8:NROW]))
                r = ROW["rwkv_mu"][0]
                ts(onemu[:, :], par[:, r:r + 14], -1.0, 1.0, ALU.mult, ALU.add)
                r = ROW["rwkv_k_a"][0]
                ts(one_k_a[:, :], par[:, r:r + NP], -1.0, 1.0, ALU.mult, ALU.add).then_inc(dve_params, 1)
                dve.wait_ge(dve_params, 2)

            def load(m, q):
                if m == 0:
                    for c in ((0, 1), (2,), (3,), ())[q]:
                        dve.wait_ge(pe_load, c + 1)
                        cp(hT[:, 2 * c:2 * c + 2, :], pair(B[c][:, :])).then_inc(dve_copy, 1)
                    dve.wait_ge(dve_copy, q + 1)
                    dve.wait_ge(dve_params, 1)
                elif q == 0:
                    dve.wait_ge(dve_params, 2)
                dve.wait_ge(act_op, 4 * m + q + 1)
                src = hT[:, 2 * q:2 * q + 2, :] if m == 0 else pair(load_bank(m, q)[:, :])
                for a in range(2):
                    k = 2 * q + a
                    last = stt(out=op_lo[m][:, k, :], in0=src[:, a, :], scalar=gain(("norm_mix", "norm_mem")[m], k),
                               in1=op_hi[m][:, k, :].bitcast(f32), op0=ALU.mult, op1=ALU.subtract)
                last.then_inc(dve_op, 1)
                if m == 0 and q % 2:
                    split_lo(q // 2)

            def diagonal_of(m):
                dve.wait_ge(act_root, m + 1)
                r = row_sum[:, 2 * m:2 * m + 2]
                link(nc.vector.reciprocal(r, r))
                for n in range(NT):
                    last = ts(diagonal[m][:, n, :], ident[:, :], row_sum[:, 2 * m + n:2 * m + n + 1], float(D), ALU.mult, ALU.mult)
                last.then_inc(dve_diag, 1)

            def spread(m):
                dve.wait_ge(pe_spread_rms, m + 1)
                cp(rinv[:, m, :], B[5][:, 0:T]).then_inc(dve_rms, 1)

            def rms(i):
                dve.wait_ge(act_rms, i - 1)
                nc.vector.reciprocal(rinv[:, 0, :], rinv[:, 0, :]).then_inc(dve_rms, 1)

            def sums():
                dve.wait_ge(act_lora, 1)
                dve.wait_ge(pool_const, 2)
                link(nc.vector.tensor_tensor_scan(out=flat(s1[:, :, :]), data0=reset, data1=flat(s0[:, :, :]),
                                                  initial=0.0, op0=ALU.mult, op1=ALU.add))
                tt(s0[:, :, :], s1[:, :, :], s0[:, :, :], ALU.subtract).then_inc(dve_sums, 1)

            def key_norm():
                dve.wait_ge(pe_kk, 1)
                ts(hsum[:, :], B[0][0:8, 0:T], 1e-24, None, ALU.max).then_inc(dve_kk, 1)
                dve.wait_ge(act_kkroot, 1)
                nc.vector.reciprocal(hsum[:, :], hsum[:, :]).then_inc(dve_kkinv, 1)

            def keys(step):
                kz, kk, rate, p_inv = flat(zT[:, 4:8, :]), flat(s4[:, :, :]), flat(s3[:, :, :]), flat(s1[:, :, :])
                q = lambda x: x[:, :, :].rearrange("p a (n t) -> p (a n) t", n=NT)
                if step == 0:
                    dve.wait_ge(pe_spread, 1)
                    for p in range(NP):
                        last = stt(out=s4[:, p, :], in0=zT[:, 4 + p, :], scalar=gain("rwkv_k_k", p),
                                   in1=B[1 + p // 2][:, (p % 2) * T:(p % 2) * T + T], op0=ALU.mult, op1=ALU.mult)
                    last.then_inc(dve_kk_all, 1)
                if step == 1:
                    dve.wait_ge(dve_kk_all, 1)
                    dve.wait_ge(act_exp, 1)
                    cp(pend[:, :, :], s2[:, :, CH - 1::CH])
                    stt(out=AR[:, :, :, 0, :].rearrange("p a n t -> p (a n) t"), in0=q(s4), scalar=-1.0,
                        in1=q(s0), op0=ALU.mult, op1=ALU.mult).then_inc(dve_A, 1)
                if step == 2:
                    dve.wait_ge(act_factor, 1)
                    tt(kz, flat(s0[:, :, :]), kz, ALU.mult)
                    link(tt(rate, kk, rate, ALU.mult))
                if step == 3:
                    tt(rate, rate, p_inv, ALU.mult)
                    tt(kk, kz, p_inv, ALU.mult).then_inc(dve_keys, 1)

            def reads():
                dve.wait_ge(dve_shift, 5)
                rz = zT[:, 0:4, :].rearrange("p a (n t) -> p (a n) t", n=NT)
                link(tt(AR[:, :, :, 1, :].rearrange("p a n t -> p (a n) t"), rz,
                        s2[:, :, :].rearrange("p a (n t) -> p (a n) t", n=NT), ALU.mult))
                for p in range(NP):
                    last = stt(out=s2[:, p, :], in0=zT[:, p, :], scalar=gain("rwkv_r_k", p), in1=zT[:, 4 + p, :],
                               op0=ALU.mult, op1=ALU.mult)
                last.then_inc(dve_reads, 1)

            def bonus():
                dve.wait_ge(pe_bonus, 1)
                for a, b in ((0, 3), (2, 0)):
                    last = stt(out=s2[:, a:a + 2, :], in0=pair(B[b][:, :]), scalar=float(HD), in1=zT[:, 8 + a:10 + a, :],
                               op0=ALU.mult, op1=ALU.mult)
                last.then_inc(dve_bonus, 1)

            def tokens():
                dve.wait_ge(pe_btok, 1)
                dve.wait_ge(dve_reads, 1)
                cp(ktok[:, 0, :], B[2][:, :])
                cp(ktok[:, 1, :], B[3][:, :]).then_inc(dve_ktok, 1)

            def mats(g):
                dve.wait_ge(pe_mats, g + 1)
                for j in range(4):
                    tt(quad(X[:, j, :]), quad(B[j][:, :]), maskX[:, :, :], ALU.mult)
                for j in range(4):
                    last = tt(neu[:, 0, j, :], B[j][:, 0:128], mask_d[:, :], ALU.mult)
                last.then_inc(dve_mats, 1)

            def nmat(g):
                dve.wait_ge(dve_mats, g + 1)
                tt(neu[:, 4, :, :], neu[:, 0, :, :], ident[:, :].unsqueeze(1).to_broadcast([128, 4, 128]), ALU.add)
                dve.wait_ge(pe_nmat, g + 1)
                for b in range(2):
                    last = tt(neu[:, 1, b::2, :], pair(B[b][:, 0:256]),
                              mask_n[:, :].unsqueeze(1).to_broadcast([128, 2, 128]), ALU.mult)
                last.then_inc(dve_nmat, 1)

            def pow2(g):
                dve.wait_ge(pe_pow2, g + 1)
                cp(neu[:, 3, :, :], quad(B[3][:, :])).then_inc(dve_pow2, 1)

            def pow4(g):
                dve.wait_ge(pe_pow4, g + 1)
                tt(neu[:, 4, :, :], quad(B[2][:, :]), neu[:, 4, :, :], ALU.add).then_inc(dve_pow4, 1)

            def pow8(g):
                dve.wait_ge(pe_pow8, g + 1)
                tt(neu[:, 4, :, :], quad(B[0][:, :]), neu[:, 4, :, :], ALU.add).then_inc(dve_pow8, 1)

            def sides(g):
                dve.wait_ge(pe_sides, g + 1)
                tt(neu[:, 4, :, :], quad(B[1][:, :]), neu[:, 4, :, :], ALU.add).then_inc(dve_inverse, 1)

            def solved(g):
                dve.wait_ge(pe_solved, g + 1)
                tt(U[:, 4 * g:4 * g + 4, :], quad(B[1][:, :]), neu[:, 0, :, :], ALU.add).then_inc(dve_solved, 1)

            def outq(g):
                dve.wait_ge(pe_outq, g + 1)
                n, p = g // 2, 2 * (g % 2)
                tt(s1[:, p:p + 2, tokens_of(n)], pair(B[3][:, 0:256]), AR[:, p:p + 2, n, 1, :], ALU.add).then_inc(dve_q, 1)

            def from_bank(b):
                return B[b][:, 0:256].rearrange("p (h v) -> p h v", h=NP)

            def psi(c):
                if c:
                    dve.wait_ge(dve_psi, c)
                    if c > 1:
                        dve.wait_ge(dve_state, c - 1)
                    link(tt(s4[:, :, 0:HD], states[:, c - 1, :, :], pend[:, :, c:c + 1].to_broadcast([128, NP, HD]), ALU.mult))
                dve.wait_ge(pe_psi, c + 1)
                if c == 0:
                    cp(states[:, 0, :, :], from_bank(3)).then_inc(dve_psi, 1)
                else:
                    tt(s4[:, :, 0:HD], from_bank(3 - c % 2), s4[:, :, 0:HD], ALU.add).then_inc(dve_psi, 1)

            def state(c):
                dve.wait_ge(dve_psi, c + 1)
                dve.wait_ge(pe_state, c)
                tt(states[:, c, :, :], from_bank(c % 2), s4[:, :, 0:HD], ALU.add).then_inc(dve_state, 1)

            def states_out():
                dve.wait_ge(pe_states_out, 1)
                for b in range(2):
                    y = s0[:, 2 * b:2 * b + 2, CH:T]
                    last = tt(y, pair(B[b][:, :])[:, :, CH:T], y, ALU.add)
                last.then_inc(dve_states_out, 1)

            def center():
                dve.wait_ge(dve_states_out, 1)
                dve.wait_ge(pe_mean, 1)
                for b in range(2):
                    y = s0[:, 2 * b:2 * b + 2, :]
                    last = stt(out=y, in0=pair(B[2 + b][:, :]), scalar=-1.0, in1=y, op0=ALU.mult, op1=ALU.add)
                last.then_inc(dve_center, 1)

            def deviation():
                dve.wait_ge(act_std, 1)
                nc.vector.reciprocal(hsum[:, :], hsum[:, :]).then_inc(dve_std, 1)

            def normalize():
                dve.wait_ge(pe_norm, 1)
                for b in range(2):
                    y = s0[:, 2 * b:2 * b + 2, :]
                    last = tt(y, pair(B[1 + b][:, :]), y, ALU.mult)
                link(last)
                for p in range(NP):
                    last = ts(s0[:, p, :], s0[:, p, :], gain("rwkv_ln_w", p), gain("rwkv_ln_b", p), ALU.mult, ALU.add)
                link(last)
                tt(s0[:, :, :], s0[:, :, :], s2[:, :, :], ALU.add).then_inc(dve_norm, 1)

            def gate():
                dve.wait_ge(dve_norm, 1)
                dve.wait_ge(pe_gate, 1)
                for b in range(2):
                    y = s0[:, 2 * b:2 * b + 2, :]
                    last = tt(y, pair(B[(0, 3)[b]][:, :]), y, ALU.mult)
                last.then_inc(dve_gate, 1)
                dve.wait_ge(act_op, 9)
                tt(op_lo[0][:, 0:4, :], s0[:, :, :], op_hi[0][:, 0:4, :].bitcast(f32), ALU.subtract).then_inc(dve_gate, 1)

            def scores(who, h):
                no = head_no(who, h)
                dve.wait_ge(pe_scores, no + 1)
                if no:
                    dve.wait_ge(pe_turn, no)
                if who == "m":
                    link(stt(out=prob[:, :, :], in0=pair(B[4][:, :]), scalar=HD ** -0.5, in1=causal[:, :, :],
                             op0=ALU.mult, op1=ALU.add))
                else:
                    link(ts(prob[:, :, :], pair(B[4][:, :]), XD ** -0.5, None, ALU.mult))
                nc.vector.reduce_max(small[:, 0:2], prob[:, :, :], AX.X, negate=True).then_inc(dve_scores, 1)

            def weigh(who, h):
                dve.wait_ge(act_prob, head_no(who, h) + 1)
                link(nc.vector.reciprocal(small[:, 4:6], small[:, 2:4]))
                tt(prob[:, :, :], prob[:, :, :], small[:, 4:6].unsqueeze(2).to_broadcast([128, NT, 256]),
                   ALU.mult).then_inc(dve_prob, 1)

            def values(who, h):
                dve.wait_ge(act_values, head_no(who, h) + 1)
                if who == "m":
                    r, k = rows(h), 4 + h // 2
                    tt(op_lo[0][r, k, :], B[4][r, 0:T], op_hi[0][r, k, :].bitcast(f32), ALU.subtract).then_inc(dve_values, 1)
                else:
                    k = slice(2 * h, 2 * h + 2)
                    tt(op_lo[1][:, k, :], pair(B[4][:, :]), op_hi[1][:, k, :].bitcast(f32), ALU.subtract)\
                        .then_inc(dve_values, 1)

            def final_rms():
                dve.wait_ge(act_root, 3)
                nc.vector.reciprocal(row_sum[:, 0:2], row_sum[:, 0:2]).then_inc(dve_rms, 1)

            def finish():
                dve.wait_ge(dve_rms, 5)
                dve.wait_ge(pe_final, 4)
                for q in range(2, 4):
                    for n in range(NT):
                        last = ts(ostage[:, n, 256 * q:256 * q + 256], B[q][:, 256 * n:256 * n + 256],
                                  row_sum[:, n:n + 1], None, ALU.mult)
                    last.then_inc(dve_final, 1)

            in_order(Parts(dense, lambda: at[0], params=params, load=load, diagonal=diagonal_of, spread=spread, rms=rms,
                           operand=operand, sums=sums, key_norm=key_norm,
                           keys=keys, reads=reads, bonus=bonus, tokens=tokens, mats=mats, nmat=nmat, pow2=pow2,
                           pow4=pow4, pow8=pow8, sides=sides, solved=solved, outq=outq, psi=psi, state=state,
                           states_out=states_out, center=center, deviation=deviation, normalize=normalize, gate=gate,
                           scores=scores, weigh=weigh, values=values, final_rms=final_rms, finish=finish))


INPUTS = ["x", "mem", "norm_mix", "w_in", "rwkv_mu", "rwkv_w0", "rwkv_w_up", "rwkv_a0", "rwkv_a_up", "rwkv_g_up",
          "rwkv_k_k", "rwkv_k_a", "rwkv_r_k", "rwkv_ln_w", "rwkv_ln_b", "w_mix_out", "norm_xattn", "norm_mem",
          "w_xq", "w_xkv", "w_xo", "norm_ffn", "w_ff1", "w_ff2", "norm_final"]


def kernel(**inputs):
    import numpy as np
    import concourse.bacc as bacc
    from concourse.bass_utils import run_bass_kernel_spmd

    nc = bacc.Bacc("TRN2", target_bir_lowering=False, num_devices=1)
    arrays, io = {}, {}
    for name in INPUTS:
        a = np.ascontiguousarray(inputs[name])
        arrays[f"in_{name}"] = a
        io[name] = nc.dram_tensor(f"in_{name}", a.shape, mybir.dt.from_np(a.dtype), kind="ExternalInput").ap()
    out = nc.dram_tensor("out", (1, T, D), mybir.dt.float32, kind="ExternalOutput").ap()
    build(nc, io, out)
    return run_bass_kernel_spmd(nc, [arrays], core_ids=[0]).results[0]["out"]
```

```python
import math
from contextlib import ExitStack

import concourse.bass as bass
from concourse import mybir

D, T, M = 1024, 256, 256
KT = D // 128
RW, NH, HD = 512, 8, 64
NP = RW // 128
CH, BLK = 32, 16
NCH = T // CH
NG = 4
DECAY = math.exp(-0.5)
GN_EPS, NORM_EPS = 64e-5, 1e-6
XH, XD = 4, 256
NF = 8
NT = T // 128
NRAW, NSPLIT = 3, 3
NEG = -1e30

PARAMS = [("norm_mix", 8), ("norm_mem", 8), ("norm_xattn", 8), ("norm_ffn", 8), ("norm_final", 8),
          ("rwkv_mu", 14), ("rwkv_w0", 4), ("rwkv_a0", 4), ("rwkv_k_k", 4), ("rwkv_k_a", 4),
          ("rwkv_r_k", 4), ("rwkv_ln_w", 4), ("rwkv_ln_b", 4)]
ROW = {}
for _n, _c in PARAMS:
    ROW[_n] = sum(c for _, c in ROW.values()), _c
NROW = sum(c for _, c in PARAMS)


def units():
    out = [("z", "w_in", 0, 256 * j, j) for j in (6, 2, 3, 0, 1, 4, 5)]
    base = 3 * RW + 256
    out += [("mq", "w_in", 0, base + 256 * j, j) for j in range(4)]
    out += [("mv", "w_in", 0, base + 2 * RW + 256 * j, j) for j in range(2)]
    out += [("xk", "w_xkv", 0, 256 * j, j) for j in range(4)]
    out += [("xv", "w_xkv", 0, D + 256 * j, j) for j in range(3)]
    out += [("mix", "w_mix_out", 0, 256 * j, j) for j in range(4)]
    out += [("xv", "w_xkv", 0, D + 256 * j, j) for j in range(3, 4)]
    out += [("xq", "w_xq", 0, 256 * j, j) for j in range(4)]
    out += [("xo", "w_xo", 0, 256 * j, j) for j in range(4)]
    for g in range(NF + 1):
        if g < NF:
            out += [("f1", "w_ff1", 0, 512 * g + 256 * j, 2 * g + j) for j in range(2)]
        if g:
            out += [("f2", "w_ff2", 4 * (g - 1), 512 * j, 2 * j) for j in range(2)]
    return out


UNITS = units()
OUTS = []
for _u, (_w, _s, _r, _c, _j) in enumerate(UNITS):
    if _w == "f2":
        OUTS += [(_u, 2 * _u + _i, 2 * _u + _i, _w, _j + _i) for _i in range(2)]
    else:
        OUTS.append((_u, 2 * _u, 2 * _u + 1, _w, _j))
OUT_OF_HALF = {_s: _o for _o, _x in enumerate(OUTS) for _s in range(_x[1], _x[2] + 1)}
FIRST = {_x[3]: _o for _o, _x in reversed(list(enumerate(OUTS)))}
KIND = {_x[3]: [_o for _o, _y in enumerate(OUTS) if _y[3] == _x[3]] for _x in OUTS}
LAST = {_x[3]: _o for _o, _x in enumerate(OUTS)}

QUARTERS = []
for _u in range(len(UNITS)):
    _late = {"mix": 0, "xo": 1, "f1": 1}.get(UNITS[_u][0])
    if UNITS[_u][4] == 0 and _late is not None:
        QUARTERS += [(2 * _u + _i, _late ^ _p ^ 1) for _i, _p in
                     ((0, 0), (2, 0), (0, 1), (1, 0), (1, 1), (2, 1), (3, 0), (3, 1))]
    elif UNITS[_u][0] in ("mv", "xv"):
        QUARTERS += [(2 * _u + _i, _p) for _p in range(2) for _i in range(2)]
    elif UNITS[_u][4] != 1 or _late is None:
        QUARTERS += [(2 * _u + _i, _p) for _i in range(2) for _p in range(2)]
BEGUN, DONE = {}, {}
for _q, (_s, _) in enumerate(QUARTERS):
    BEGUN.setdefault(_s, _q)
    DONE[_s] = _q
ENDS = {DONE[_x[2]]: _o for _o, _x in enumerate(OUTS)}
AFTER = {_q + (0 if _o == LAST["f2"] else 1): _o for _q, _o in ENDS.items()}


def nth(o):
    return sum(x[3] == OUTS[o][3] for x in OUTS[:o])


POOL_SPLITS = [*range(3, 12, 2), *range(21, 2 * OUTS[FIRST["mix"]][0], 2)]


def rests(s):
    pool = sum(x <= s for x in POOL_SPLITS)
    return s + 1 - pool, pool


FILL_START = 3
FILL_EARLY = 3, 2, 1, 1, 4, 1, 1, 0, 0, 1, 0, 2, 1, 2, 3, 3, 3, 2
FILL_GROUP = ((1, 1, 0, 1, 1, 1, 0, 1, 1, 1),
              (2, 1, 1, 1, 1, 1, 2, 1, 1, 1),
              (0, 0, 0, 1, 1, 1, 0, 0, 0, 0),
              (3, 0, 0, 1, 0, 1, 1, 0, 0, 1))
FILL_PHI = 1, 1
FILL_STATE = 0, 1, 2, 1, 1, 2, 1
FILL_END = 2, 1, 1, 0, 0
FILL_MIX = 1, 0, 1, 0
FILL_CROSS = (1, 3, 0, 1), (2, 1, 1, 1), (1, 2, 1, 1), (0, 1, 1, 1), (1, 1, 0, 0)


def in_order(do):
    step = [0]

    def moba():
        i, part = divmod(step[0], 3)
        step[0] += 1
        if part == 0:
            if 0 < i <= NH:
                do.weigh("m", i - 1)
            if 2 <= i < NH + 2:
                do.values("m", i - 2)
        elif part == 1 and 0 < i <= NH:
            do.turn("m", i - 1)
        elif part == 2 and i < NH:
            do.scores("m", i)

    do.params(0)
    for q in range(KT // 2):
        do.load(0, q)
    do.stats(0)
    do.diagonal(0)
    do.params(1)
    early = (do.spread, 0), (do.gates,), (do.lora,), (do.rates,), (do.sums,), (do.key_sums,), (do.key_norm,), \
        (do.stats, 1), (do.decays,), (do.keys, 0), (do.diagonal, 1), (do.keys, 1), (do.spread, 1), (do.keys, 2), \
        (do.keys, 3), (do.reads,), (do.tokens,), (do.bonus,)
    do.dense(FILL_START)
    for (stage, *index), n in zip(early, FILL_EARLY):
        stage(*index)
        do.dense(n)
    for g in range(NG):
        for n, stage in enumerate((do.mats, do.nmat, do.pow2, do.pow4, do.pow8, do.sides, do.solve, do.carry,
                                   do.solved, do.outq)):
            stage(g)
            if g >= 2:
                moba()
            do.dense(FILL_GROUP[g][n])
            if g == 0 and n in (2, 4, 6, 8):
                do.load(1, n // 2 - 1)
    do.phi(0)
    do.dense(FILL_PHI[0])
    do.phi(1)
    do.dense(FILL_PHI[1])
    for c in range(NCH - 1):
        do.psi(c)
        if c:
            moba()
            do.state(c)
        do.dense(FILL_STATE[c])
    for stage, n in zip((do.states_out, do.center, do.deviation, do.normalize, do.gate), FILL_END):
        stage()
        do.dense(n)
    while step[0] < 3 * (NH + 2):
        moba()
    do.dense(PHASE["mix"] - do.at())
    for j in range(4):
        if j == 3:
            do.rms(2)
        do.dense(FILL_MIX[j])
        do.operand("mix", j)
    for i in range(XH + 1):
        do.dense(FILL_CROSS[i][0])
        if i >= 2:
            do.turn("x", i - 2)
        if i:
            do.scores("x", i - 1)
        do.dense(FILL_CROSS[i][1])
        if i:
            do.weigh("x", i - 1)
        do.dense(FILL_CROSS[i][2])
        if i >= 2:
            do.values("x", i - 2)
        do.dense(FILL_CROSS[i][3])
    do.turn("x", XH - 1)
    do.values("x", XH - 1)
    do.dense(PHASE["xo"] - do.at())
    do.dense(4)
    do.rms(3)
    do.dense(PHASE["f2"] - do.at())
    do.final_rms()
    do.finish()


PHASE = {_x[3]: 2 * (_x[2] + 1) for _x in OUTS}


class Parts:

    def __init__(self, dense, at, **parts):
        self.dense, self.at = dense, at
        skip = lambda *index: None
        self.params = parts.get("params", skip)
        self.load, self.rms = parts.get("load", skip), parts.get("rms", skip)
        self.stats, self.spread = parts.get("stats", skip), parts.get("spread", skip)
        self.diagonal, self.rates = parts.get("diagonal", skip), parts.get("rates", skip)
        self.gates, self.lora = parts.get("gates", skip), parts.get("lora", skip)
        self.sums, self.decays = parts.get("sums", skip), parts.get("decays", skip)
        self.key_sums = parts.get("key_sums", skip)
        self.key_norm, self.keys = parts.get("key_norm", skip), parts.get("keys", skip)
        self.reads, self.bonus = parts.get("reads", skip), parts.get("bonus", skip)
        self.tokens = parts.get("tokens", skip)
        self.mats, self.nmat = parts.get("mats", skip), parts.get("nmat", skip)
        self.pow2, self.pow4, self.pow8 = (parts.get(n, skip) for n in ("pow2", "pow4", "pow8"))
        self.sides, self.solve = parts.get("sides", skip), parts.get("solve", skip)
        self.carry, self.solved = parts.get("carry", skip), parts.get("solved", skip)
        self.outq, self.phi = parts.get("outq", skip), parts.get("phi", skip)
        self.psi, self.state = parts.get("psi", skip), parts.get("state", skip)
        self.states_out, self.center = parts.get("states_out", skip), parts.get("center", skip)
        self.deviation, self.normalize = parts.get("deviation", skip), parts.get("normalize", skip)
        self.operand = parts.get("operand", skip)
        self.final_rms = parts.get("final_rms", skip)
        self.gate, self.finish = parts.get("gate", skip), parts.get("finish", skip)
        self.scores, self.weigh = parts.get("scores", skip), parts.get("weigh", skip)
        self.turn, self.values = parts.get("turn", skip), parts.get("values", skip)


def build(nc, io, out):
    f32, f32r = mybir.dt.float32, mybir.dt.float32r
    ALU, ACT, AX = mybir.AluOpType, mybir.ActivationFunctionType, mybir.AxisListType
    ctx = ExitStack()
    with ctx:
        def sb(name, shape, dt=f32):
            return ctx.enter_context(nc.sbuf_tensor(name, shape, dt))

        def sem(name):
            return ctx.enter_context(nc.semaphore(name))

        def flat(x):
            return x.rearrange("p a t -> p (a t)")

        def by_token(x):
            return flat(x).rearrange("p (n c) -> p n c", n=NT)

        raw = sb("raw", [128, NRAW, 8 * 256])
        w_hi = sb("w_hi", [128, NSPLIT, 1024], f32r)
        w_lo = sb("w_lo", [128, NSPLIT, 1024], f32r)
        op_hi = [sb(f"op{i}_hi", [128, KT, T], f32r) for i in range(2)]
        op_lo = [sb(f"op{i}_lo", [128, KT, T], f32r) for i in range(2)]
        hT = sb("hT", [128, KT, T])
        rinv = sb("rinv", [128, 2, T])
        tmp = sb("tmp", [128, 2, 512])
        zT = sb("zT", [128, 14, T])
        mqk = sb("mqk", [128, 8, T])
        mval = sb("mval", [128, NT, RW])
        xkey = sb("xkey", [128, KT, M])
        xval = sb("xval", [128, NT, D])
        prob = sb("prob", [128, NT, 256])
        probT = sb("probT", [128, NT, 256])
        small = sb("small", [128, 16])
        s0 = sb("s0", [128, NP, T])
        s1 = sb("s1", [128, NP, T])
        s2 = sb("s2", [128, NP, T])
        s3 = sb("s3", [128, NP, T])
        s4 = sb("s4", [128, NP, T])
        AR = sb("AR", [128, NP, NT, 2, 128])
        btok = sb("btok", [128, NT, RW])
        U = sb("U", [128, 2 * NH, 128])
        X = sb("X", [128, 4, 512])
        neu = sb("neu", [128, 5, 4, 128])
        pend = sb("pend", [128, NP, NCH])
        par = sb("par", [128, NROW])
        onemu = sb("onemu", [128, 14])
        ident = sb("ident", [128, 128])
        ones = sb("ones", [128, 128])
        hblock = sb("hblock", [128, 128])
        maskX = sb("maskX", [128, 4, 128])
        mask_d = sb("mask_d", [128, 128])
        mask_n = sb("mask_n", [128, 128])
        causal = sb("causal", [128, NT, 256])
        ind = sb("ind", [128, NP, 8])
        indT = sb("indT", [8, NP, 128])
        eps = sb("eps", [128, 2])
        row_sum = sb("row_sum", [128, 4])
        one_k_a = sb("one_k_a", [128, NP])
        ktok, vtok = by_token(zT[:, 4:8, :]), by_token(zT[:, 0:4, :])
        prow = prob[:, 0, 0:128]
        stage = [xval, by_token(xkey[:, :, :])]
        reset = flat(X[:, :, :])[:, 0:NP * T]
        PHI = flat(X[:, :, :])[:, 0:6 * 256].rearrange("p (c h k) -> p c h k", c=6, h=NP)
        states = neu[:, :, :, :].rearrange("p a b c -> p (a b c)")[:, 0:7 * 256]\
            .rearrange("p (c h k) -> p c h k", c=7, h=NP)
        hsum = zT[0:8, 12, :]
        lora_up = flat(U[:, 0:4, :])
        gate_up = AR[:, 0, :, :, :].rearrange("p n a t -> p (n a t)")
        xqT = zT[:, 0:8, :]
        sq_out = neu[:, :, :, :].rearrange("p a b c -> p (a b c)")[:, 0:D]
        diagonal = [x.rearrange("p (n c) -> p n c", n=NT) for x in (prob[:, 1, :], probT[:, 0, :])]
        square, square_sum = s1[:, 0:2, :], s2[:, 0:2, :]
        ostage = by_token(xkey[:, :, :])

        bank = [ctx.enter_context(nc.psum_tensor(f"bank{i}", [128, 512], f32)) for i in range(8)]
        B, dense_bank = bank[0:6], bank[6:8]

        raw_in = [sem(f"raw_in{i}") for i in range(NRAW)]
        x_in, mem_in, mix_in = [sem("x_in0"), sem("x_in1")], sem("mem_in"), sem("mix_in")
        act_sums, act_root, dve_diag, pe_spread_rms = sem("act_sums"), sem("act_root"), sem("dve_diag"), sem("pe_spread_rms")
        dve_copy, act_rest, act_factor, pool_tails, pool_R = sem("dve_copy"), sem("act_rest"), sem("act_factor"), sem("pool_tails"), sem("pool_R")
        params_in, lora_in, gate_in, out_done = sem("params_in"), sem("lora_in"), sem("gate_in"), sem("out_done")
        hi_done, lo_done, pool_lo, dense_mm, out_taken = sem("hi_done"), sem("lo_done"), sem("pool_lo"), sem("dense_mm"), sem("out_taken")
        pool_const, pool_link, act_link, dve_link = sem("pool_const"), sem("pool_link"), sem("act_link"), sem("dve_link")
        pe_params, dve_params = sem("pe_params"), sem("dve_params")
        pe_load, act_op, dve_op = sem("pe_load"), sem("act_op"), sem("dve_op")
        pe_square, act_square, pool_square = sem("pe_square"), sem("act_square"), sem("pool_square")
        act_rms, dve_rms = sem("act_rms"), sem("dve_rms")
        act_hidden, dve_hidden = sem("act_hidden"), sem("dve_hidden")
        dve_shift, act_gates, pe_lora, act_lora = sem("dve_shift"), sem("act_gates"), sem("pe_lora"), sem("act_lora")
        dve_sums, act_exp = sem("dve_sums"), sem("act_exp")
        act_kk, pe_kk, dve_kk, act_kkroot, dve_kkinv = sem("act_kk"), sem("pe_kk"), sem("dve_kk"), sem("act_kkroot"), sem("dve_kkinv")
        pe_spread, dve_kk_all, dve_A, dve_B = sem("pe_spread"), sem("dve_kk_all"), sem("dve_A"), sem("dve_B")
        dve_keys, dve_reads = sem("dve_keys"), sem("dve_reads")
        pe_bonus, dve_bonus = sem("pe_bonus"), sem("dve_bonus")
        pe_btok, act_btok, dve_ktok, pe_vtok, act_vtok = sem("pe_btok"), sem("act_btok"), sem("dve_ktok"), sem("pe_vtok"), sem("act_vtok")
        pe_mats, dve_mats, pe_nmat, dve_nmat = sem("pe_mats"), sem("dve_mats"), sem("pe_nmat"), sem("dve_nmat")
        pe_pow2, act_pow2, dve_pow2 = sem("pe_pow2"), sem("act_pow2"), sem("dve_pow2")
        pe_pow4, act_pow4, dve_pow4 = sem("pe_pow4"), sem("act_pow4"), sem("dve_pow4")
        pe_pow8, act_pow8, dve_pow8 = sem("pe_pow8"), sem("act_pow8"), sem("dve_pow8")
        pe_sides, act_sides, dve_inverse = sem("pe_sides"), sem("act_sides"), sem("dve_inverse")
        pe_solve, act_solve, pe_carry, act_carry = sem("pe_solve"), sem("act_solve"), sem("pe_carry"), sem("act_carry")
        pe_solved, dve_solved = sem("pe_solved"), sem("dve_solved")
        pe_outq, act_out, dve_q = sem("pe_outq"), sem("act_out"), sem("dve_q")
        pe_phi, act_phi = sem("pe_phi"), sem("act_phi")
        pe_psi, dve_psi, pe_state, dve_state = sem("pe_psi"), sem("dve_psi"), sem("pe_state"), sem("dve_state")
        pe_states_out, dve_states_out = sem("pe_states_out"), sem("dve_states_out")
        pe_mean, dve_center, act_dev = sem("pe_mean"), sem("dve_center"), sem("act_dev")
        pe_var, act_std, dve_std = sem("pe_var"), sem("act_std"), sem("dve_std")
        pe_norm, dve_norm, pe_gate, act_gate, dve_gate = (
            sem(n) for n in ("pe_norm", "dve_norm", "pe_gate", "act_gate", "dve_gate"))
        pe_scores, dve_scores, act_prob, dve_prob = sem("pe_scores"), sem("dve_scores"), sem("act_prob"), sem("dve_prob")
        pe_turn, act_turn, pe_values, act_values, dve_values = (
            sem(n) for n in ("pe_turn", "act_turn", "pe_values", "act_values", "dve_values"))
        dve_ln_b, dve_gain, dve_final, pe_final, act_final = sem("dve_ln_b"), sem("dve_gain"), sem("dve_final"), sem("pe_final"), sem("act_final")

        def gain(name, k):
            return par[:, ROW[name][0] + k:ROW[name][0] + k + 1]

        def pair(x):
            return x.rearrange("p (a t) -> p a t", a=2)

        def quad(x):
            return x.rearrange("p (a t) -> p a t", a=4)

        def rows(h):
            return slice(HD * (h % 2), HD * (h % 2) + HD)

        def cols(h):
            return slice(HD * h, HD * h + HD)

        def unit_of(g, j):
            return g // 2, 4 * (g % 2) + j

        def tokens_of(n):
            return slice(128 * n, 128 * n + 128)

        def split_views(s):
            u, i = divmod(s, 2)
            k, n = (4, 256) if UNITS[u][0] == "f2" else (8, 128)
            r = raw[:, u % NRAW, :].rearrange("p (k c) -> p k c", k=k)[:, :, n * i:n * i + n]
            if UNITS[u][0] in ("mv", "xv"):
                k, r = 4, raw[:, u % NRAW, :].rearrange("p (k c) -> p k c", k=8)[:, 4 * i:4 * i + 4, :]
            return r, lambda w: w[:, s % NSPLIT, :].rearrange("p (k c) -> p k c", k=k)

        def head_no(who, h):
            return h if who == "m" else NH + h

        def reach(who, n):
            return 128 if who == "m" and n == 0 else 256

        def op_no(what, j):
            return {"x": 0, "mem": 4, "mix": 8, "xo": 12}[what] + j

        def load_bank(m, q):
            return B[q] if m == 0 else B[4 + q % 2]

        block = ctx.enter_context(nc.Block())

        @block.sync
        def _(sp):
            sp.dma_start(prow[0:8, :], io["norm_mix"].rearrange("l (r p) -> (l r) p", p=128)).then_inc(mix_in, 16)
            x = io["x"].rearrange("b (n p) d -> p (b n) d", p=128)
            for half in range(2):
                c = slice(512 * half, 512 * half + 512)
                sp.dma_start(stage[0][:, :, c], x[:, :, c]).then_inc(x_in[half], 16)

            def load_unit(u):
                what, src, r, c, _ = UNITS[u]
                if u >= NRAW:
                    sp.wait_ge(hi_done, 2 * (u - NRAW) + 2)
                    by_dve, by_pool = rests(2 * (u - NRAW) + 1)
                    sp.wait_ge(lo_done, by_dve)
                    if by_pool:
                        sp.wait_ge(pool_lo, by_pool)
                w = io[src].rearrange("l (k p) n -> p (l k) n", p=128)
                k, n = (4, 512) if what == "f2" else (8, 256)
                sp.dma_start(raw[:, u % NRAW, :].rearrange("p (k c) -> p k c", k=k),
                             w[:, r:r + k, c:c + n]).then_inc(raw_in[u % NRAW], 16)

            load_unit(0)
            for name, (r, c) in ROW.items():
                if name != "norm_mix":
                    v = io[name]
                    v = v.rearrange("l h d -> (l h d)") if len(v.shape) == 3 else \
                        v.rearrange("l d -> (l d)") if len(v.shape) == 2 else v
                    sp.dma_start(prow[r:r + c, :], v.rearrange("(r p) -> r p", p=128)).then_inc(params_in, 16)
            sp.dma_start(lora_up[0:64, :], io["rwkv_w_up"].rearrange("l r c -> (l r) c")).then_inc(lora_in, 16)
            sp.dma_start(lora_up[64:128, :], io["rwkv_a_up"].rearrange("l r c -> (l r) c")).then_inc(lora_in, 16)
            sp.dma_start(stage[1], io["mem"].rearrange("b (n p) d -> p (b n) d", p=128)).then_inc(mem_in, 16)
            for u in range(1, len(UNITS)):
                load_unit(u)
            o = out.rearrange("b (n p) d -> p (b n) d", p=128)
            for q, (done, count) in enumerate(((act_final, 1), (act_final, 2), (dve_final, 1), (dve_final, 2))):
                sp.wait_ge(done, count)
                sp.dma_start(o[:, :, 256 * q:256 * q + 256], ostage[:, :, 256 * q:256 * q + 256]).then_inc(out_done, 16)
            sp.wait_ge(out_done, 64)

        @block.gpsimd
        def _(pool):
            n = [0]

            def link(ins):
                n[0] += 1
                ins.then_inc(pool_link, 1)
                pool.wait_ge(pool_link, n[0])

            def select(ap, pattern, base, cm, op=ALU.is_ge, fill=0.0):
                link(nc.gpsimd.affine_select(out=ap, in_=ap, compare_op=op, fill=fill, base=base,
                                             pattern=pattern, channel_multiplier=cm))

            link(nc.gpsimd.memset(ident[:, :], 0.0))
            select(ident[:, :], [[-1, 128]], 0, 1, ALU.not_equal, 1.0)
            nc.gpsimd.memset(eps[:, 0:1], NORM_EPS)
            nc.gpsimd.memset(ones[:, :], 1.0 / D).then_inc(pool_const, 1)
            for t, v in ((hblock, 1.0 / HD), (maskX, 1.0), (mask_d, 1.0), (mask_n, 1.0), (ind, 1.0), (indT, 1.0),
                         (causal, 0.0)):
                nc.gpsimd.memset(t[:], v)
            nc.gpsimd.memset(reset, 1.0)
            link(nc.gpsimd.memset(eps[:, 1:2], GN_EPS))
            link(nc.gpsimd.memset(reset.rearrange("p (c t) -> p c t", t=CH)[:, :, 0:1], 0.0))
            hb = hblock[:, :].rearrange("p (b k) -> p b k", b=2)
            select(hb, [[-HD, 2], [0, HD]], 0, 1)
            select(hb, [[HD, 2], [0, HD]], HD - 1, -1)
            select(ind[:, :, :], [[128, NP], [-HD, 8]], 0, 1)
            select(ind[:, :, :], [[-128, NP], [HD, 8]], HD - 1, -1)
            it = indT[:, :, :].rearrange("j n (b k) -> j n b k", b=2)
            select(it, [[-2, NP], [-1, 2], [0, HD]], 0, 1, ALU.is_equal)
            for part in range(4):
                m = maskX[:, part, :]
                select(m, [[1, 128]], 0 if part % 2 else -1, -1)
                select(m.rearrange("p (c r) -> p c r", r=CH), [[-CH, 128 // CH], [0, CH]], 0, 1)
            for m, sign in ((mask_d, -1), (mask_n, 1)):
                select(m[:, :], [[-sign, 128]], -1, sign)
                mb = m[:, :].rearrange("p (c r) -> p c r", r=BLK)
                select(mb, [[-BLK, 128 // BLK], [0, BLK]], 0, 1)
                select(mb, [[BLK, 128 // BLK], [0, BLK]], BLK - 1, -1)
            link(nc.gpsimd.tensor_tensor(maskX[:, 0, :], maskX[:, 0, :], mask_d[:, :], ALU.subtract))
            nc.gpsimd.affine_select(out=causal[:, :, :], in_=causal[:, :, :], compare_op=ALU.is_ge, fill=NEG, base=0,
                                    pattern=[[128, NT], [-1, 256]], channel_multiplier=1).then_inc(pool_const, 1)

            def split_lo(s):
                pool.wait_ge(hi_done, s + 1)
                r, view = split_views(s)
                nc.gpsimd.tensor_tensor(view(w_lo), r, view(w_hi).bitcast(f32), ALU.subtract).then_inc(pool_lo, 1)

            for s in POOL_SPLITS[:5]:
                split_lo(s)
            pool.wait_ge(dve_A, 1)
            pool.wait_ge(dve_shift, 5)
            nc.gpsimd.tensor_tensor(AR[:, :, :, 1, :].rearrange("p a n t -> p (a n) t"),
                                    zT[:, 0:4, :].rearrange("p a (n t) -> p (a n) t", n=NT),
                                    s2[:, :, :].rearrange("p a (n t) -> p (a n) t", n=NT), ALU.mult).then_inc(pool_R, 1)
            pool.wait_ge(dve_keys, 1)
            at_end = pend[:, :, :].rearrange("p a c -> p (a c)").unsqueeze(2).to_broadcast([128, NP * NCH, CH])
            nc.gpsimd.tensor_tensor(s0[:, :, :].rearrange("p a (c t) -> p (a c) t", t=CH),
                                    s3[:, :, :].rearrange("p a (c t) -> p (a c) t", t=CH), at_end, ALU.mult)
            nc.gpsimd.tensor_tensor(s1[:, :, :].rearrange("p a (c t) -> p (a c) t", t=CH),
                                    s4[:, :, :].rearrange("p a (c t) -> p (a c) t", t=CH), at_end, ALU.mult)\
                .then_inc(pool_tails, 1)
            for s in POOL_SPLITS[5:]:
                split_lo(s)
            pool.wait_ge(dve_q, NG)
            pool.dma_start(gate_up, io["rwkv_g_up"].rearrange("l r c -> (l r) c")).then_inc(gate_in, 16)
            for count, what in enumerate(("mix", "xo")):
                for j in range(4):
                    pool.wait_ge(out_taken, FIRST[what] + j + 1)
                    if j == 0 and count:
                        pool.wait_ge(pe_square, 1)
                    h = hT[:, 2 * j:2 * j + 2, :]
                    if j == 0:
                        link(nc.gpsimd.tensor_tensor(square_sum, h, h, ALU.mult))
                        continue
                    link(nc.gpsimd.tensor_tensor(square, h, h, ALU.mult))
                    last = nc.gpsimd.tensor_tensor(square_sum, square_sum, square, ALU.add)
                    if j < 3:
                        link(last)
                last.then_inc(pool_square, 1)

        @block.tensor
        def _(pe):
            mm, turn_op = nc.tensor.matmul, nc.tensor.transpose
            pe.wait_ge(pool_const, 1)
            at = [0]

            def quarter(q):
                s, part = QUARTERS[q]
                what, _, r, _, _ = UNITS[s // 2]
                o = OUT_OF_HALF[s]
                deep = what == "f2"
                if q == BEGUN[s]:
                    if s == OUTS[o][1] and o >= 2:
                        pe.wait_ge(out_taken, o - 1)
                    pe.wait_ge(hi_done, s + 1)
                    by_dve, by_pool = rests(s)
                    if s in POOL_SPLITS:
                        pe.wait_ge(pool_lo, by_pool)
                    else:
                        pe.wait_ge(lo_done, by_dve)
                which = 1 if what in ("xk", "xv", "xo", "f2") else 0
                opening = o - FIRST[what] <= (what in ("xo", "f1")) and s == OUTS[o][1] and not deep
                if what == "mix" and q == BEGUN[s] and s == OUTS[FIRST[what]][1]:
                    pe.wait_ge(dve_values, NH)
                if deep and s % 4 == 0 and q == BEGUN[s]:
                    pe.wait_ge(dve_hidden, 2 * (r // 4) + 2)
                b = dense_bank[o % 2]
                _, view = split_views(s)
                wh, wl = view(w_hi), view(w_lo)
                if what in ("mv", "xv"):
                    dst = b[:, 256 * part:256 * part + 256]
                    for k in range(4):
                        xk = 4 * (s % 2) + k
                        hi, lo = op_hi[which][:, xk, tokens_of(part)], op_lo[which][:, xk, tokens_of(part)]
                        mm(dst, hi, wh[:, k, :], start=(xk == 0), stop=False)
                        mm(dst, hi, wl[:, k, :], start=False, stop=False)
                        last = mm(dst, lo, wh[:, k, :], start=False, stop=(xk == KT - 1))
                    if q == DONE[s]:
                        last.then_inc(dense_mm, 1)
                    if q in AFTER:
                        follow(AFTER[q])
                    return
                if deep:
                    todo = [(k, 4 * (r // 4 % 2) + k, 128 * part, part * T, k == 0, k == 3) for k in range(4)]
                else:
                    todo = [(k, k, 0, (s % 2) * T, q == BEGUN[s] and k % 4 == 0, q == DONE[s] and k % 4 == 3)
                            for k in range(4 * part, 4 * part + 4)]
                for k, xk, c, t, first, final in todo:
                    if what == "mix" and s == OUTS[FIRST[what]][1] and k in (0, 2):
                        pe.wait_ge(dve_gate, 3 + k // 2)
                    if opening and what == "xo" and k % 2 == 0:
                        pe.wait_ge(dve_values, NH + k // 2 + 1)
                    if opening and what in ("z", "xk", "xq", "f1") and k % 2 == 0:
                        pe.wait_ge(dve_op, op_no({"z": "x", "xk": "mem", "xq": "mix", "f1": "xo"}[what], k // 2) + 1)
                    dst = b[:, t:t + T]
                    mm(dst, wh[:, k, c:c + 128], op_hi[which][:, xk, :], start=first, stop=False)
                    mm(dst, wh[:, k, c:c + 128], op_lo[which][:, xk, :], start=False, stop=False)
                    last = mm(dst, wl[:, k, c:c + 128], op_hi[which][:, xk, :], start=False, stop=final)
                if q == DONE[s]:
                    last.then_inc(dense_mm, 1)
                if q in AFTER:
                    follow(AFTER[q])

            def follow(o):
                if OUTS[o][3] == "f2" and o >= len(OUTS) - 4:
                    squares(o - len(OUTS) + 4)
                    turn_out(o - len(OUTS) + 4)

            def dense(n):
                for q in range(at[0], at[0] + n):
                    quarter(q)
                at[0] += n

            bank5 = [None]

            def squares(j):
                pe.wait_ge(act_square, j + 1)
                if j == 0:
                    pe.wait_ge(act_rms, 2)
                for n in range(NT):
                    for a in range(2):
                        last = mm(B[4 + n][:, 0:1], tmp[:, 1, a * T + 128 * n:a * T + 128 * n + 128], ones[:, 0:1],
                                  start=(j == 0 and a == 0), stop=(j == 3 and a == 1))
                last.then_inc(pe_square, 1)

            def turn_out(j):
                pe.wait_ge(dve_gain, j + 1)
                for n in range(NT):
                    for a in range(2):
                        last = turn_op(B[j][:, 256 * n + 128 * a:256 * n + 128 * a + 128],
                                       zT[:, 2 * j + a, tokens_of(n)], ident[:, :])
                last.then_inc(pe_final, 1)

            def params(part):
                if part == 0:
                    pe.wait_ge(mix_in, 16)
                    turn_op(B[4][:, 0:8], prow[0:8, :], ident[0:8, 0:8]).then_inc(pe_params, 1)
                else:
                    pe.wait_ge(params_in, 16 * (len(PARAMS) - 1))
                    pe.wait_ge(dve_params, 1)
                    turn_op(B[4][:, 0:NROW], prow[0:NROW, :], ident[0:NROW, 0:NROW]).then_inc(pe_params, 1)

            def load(m, q):
                if m == 0:
                    pe.wait_ge(x_in[q // 2], 16)
                elif q == 0:
                    pe.wait_ge(mem_in, 16)
                b = load_bank(m, q)
                if m and q == 0:
                    pe.wait_ge(dve_params, 2)
                    pe.wait_ge(dve_rms, 2)
                if m and q >= 2:
                    pe.wait_ge(dve_op, 4 + q - 1)
                for a in range(2):
                    for n in range(NT):
                        last = turn_op(b[:, 256 * a + 128 * n:256 * a + 128 * n + 128],
                                       stage[m][:, n, 256 * q + 128 * a:256 * q + 128 * a + 128], ident[:, :])
                last.then_inc(pe_load, 1)
                if (m, q) == (1, 3):
                    bank5[0] = dve_op, 8

            def spread(m):
                pe.wait_ge(dve_diag, m + 1)
                if m:
                    pe.wait_ge(dve_rms, 1)
                for n in range(NT):
                    last = mm(B[5][:, tokens_of(n)], ones[:, :], diagonal[m][:, n, :], start=True, stop=True)
                last.then_inc(pe_spread_rms, 1)
                bank5[0] = dve_rms, m + 1

            def rms(i):
                if i in (2, 3):
                    pe.wait_ge(pool_square, i - 1)
                    if bank5[0]:
                        pe.wait_ge(*bank5[0])
                    for a in range(2):
                        last = mm(B[5][:, 0:T], ones[:, :], square_sum[:, a, :], start=(a == 0), stop=(a == 1))
                    last.then_inc(pe_square, 1)
                bank5[0] = act_rms, i - 1

            def lora():
                pe.wait_ge(lora_in, 32)
                pe.wait_ge(act_gates, 1)
                pe.wait_ge(dve_op, 4)
                for lo in (0, 64):
                    for p in range(NP):
                        last = mm(B[lo // 32 + p // 2][:, (p % 2) * T:(p % 2) * T + T],
                                  lora_up[lo:lo + 64, tokens_of(p)], zT[lo:lo + 64, 12, :], start=True, stop=True)
                last.then_inc(pe_lora, 1)

            def head_sums(src, signal):
                for p in range(NP):
                    last = mm(B[0][0:8, 0:T], ind[:, p, :], src[:, p, :], start=(p == 0), stop=(p == NP - 1))
                last.then_inc(signal, 1)

            def by_pair(banks, lhs, rhs, signal):
                for p in range(NP):
                    last = mm(B[banks[p // 2]][:, (p % 2) * T:(p % 2) * T + T], lhs(p), rhs(p), start=True, stop=True)
                last.then_inc(signal, 1)

            def key_sums():
                pe.wait_ge(pool_const, 2)
                pe.wait_ge(act_kk, 1)
                pe.wait_ge(act_lora, 1)
                head_sums(s4, pe_kk)

            def keys(step):
                if step:
                    return
                pe.wait_ge(dve_kkinv, 1)
                by_pair((1, 2), lambda p: indT[:, p, :], lambda p: hsum[:, :], pe_spread)

            def tokens():
                pe.wait_ge(pool_tails, 1)
                pe.wait_ge(dve_kk_all, 1)
                for src, b in ((s0, 0), (s1, 2)):
                    for n in range(NT):
                        for p in range(NP):
                            last = turn_op(B[b + n][:, tokens_of(p)], src[:, p, tokens_of(n)], ident[:, :])
                last.then_inc(pe_btok, 1)

            def bonus():
                pe.wait_ge(dve_shift, 7)
                pe.wait_ge(act_btok, 1)
                pe.wait_ge(dve_ktok, 1)
                for n in range(NT):
                    for p in range(NP):
                        last = turn_op(B[1 + n][:, tokens_of(p)], zT[:, 8 + p, tokens_of(n)], ident[:, :])
                last.then_inc(pe_vtok, 1)
                pe.wait_ge(dve_reads, 1)
                by_pair((3, 0), lambda p: hblock[:, :], lambda p: s2[:, p, :], pe_bonus)

            def mats(g):
                if g == 0:
                    pe.wait_ge(act_vtok, 1)
                    pe.wait_ge(dve_bonus, 1)
                else:
                    pe.wait_ge(act_out, g)
                    pe.wait_ge(dve_q, g)
                for j in range(4):
                    n, h = unit_of(g, j)
                    both = AR[rows(h), h // 2, n, :, :].rearrange("p a t -> p (a t)")
                    mm(B[j][:, 0:256], s3[rows(h), h // 2, tokens_of(n)], both, start=True, stop=True)
                    last = mm(B[j][:, 256:512], s4[rows(h), h // 2, tokens_of(n)], both, start=True, stop=True)
                last.then_inc(pe_mats, 1)

            def nmat(g):
                pe.wait_ge(dve_mats, 2 * g + 1)
                for j in range(4):
                    n, h = unit_of(g, j)
                    last = mm(B[j % 2][:, tokens_of(j // 2)], AR[rows(h), h // 2, n, 0, :],
                              s3[rows(h), h // 2, tokens_of(n)], start=True, stop=True)
                last.then_inc(pe_nmat, 1)

            def four(b, lhs, rhs):
                for j in range(4):
                    last = mm(B[b][:, tokens_of(j)], neu[:, lhs, j, :], neu[:, rhs, j, :], start=True, stop=True)
                return last

            def pow2(g):
                pe.wait_ge(dve_nmat, g + 1)
                four(2, 1, 0)
                four(3, 0, 1).then_inc(pe_pow2, 1)

            def pow4(g):
                pe.wait_ge(act_pow2, g + 1)
                pe.wait_ge(dve_pow2, g + 1)
                four(0, 3, 2)
                four(1, 2, 3)
                four(2, 3, 4).then_inc(pe_pow4, 1)

            def pow8(g):
                pe.wait_ge(act_pow4, g + 1)
                pe.wait_ge(dve_pow4, g + 1)
                four(3, 0, 1)
                four(0, 1, 4).then_inc(pe_pow8, 1)

            def sides(g):
                w = B[2][:, :].rearrange("p (j x k) -> p j x k", j=4, x=2)
                for j in range(4):
                    n, h = unit_of(g, j)
                    mm(w[:, j, 0, :], X[:, j, 256:384], vtok[:, n, cols(h)], start=True, stop=True)
                for j in (0, 2):
                    n, h = unit_of(g, j)
                    turn_op(w[:, j:j + 2, 1, :], AR[:, h // 2, n, 0, :], ident[:, :])
                pe.wait_ge(act_pow8, g + 1)
                pe.wait_ge(dve_pow8, g + 1)
                four(1, 2, 4).then_inc(pe_sides, 1)

            def solve(g):
                pe.wait_ge(act_sides, g + 1)
                pe.wait_ge(dve_inverse, g + 1)
                four(3, 4, 3).then_inc(pe_solve, 1)

            def carry(g):
                pe.wait_ge(act_solve, g + 1)
                for j in range(4):
                    last = mm(B[0][:, tokens_of(j)], X[:, j, 0:128], neu[:, 0, j, :], start=True, stop=True)
                last.then_inc(pe_carry, 1)

            def solved(g):
                pe.wait_ge(act_carry, g + 1)
                four(1, 4, 1).then_inc(pe_solved, 1)

            def outq(g):
                pe.wait_ge(act_solve, g + 1)
                for j in range(4):
                    n, h = unit_of(g, j)
                    mm(B[2][rows(h), tokens_of(j // 2)], vtok[:, n, cols(h)], X[:, j, 384:512], start=True, stop=False)
                    if j == 0:
                        pe.wait_ge(dve_solved, g + 1)
                    mm(B[2][rows(h), tokens_of(j // 2)], U[:, 4 * g + j, 0:HD], X[:, j, 128:256], start=False, stop=True)
                for j in range(4):
                    last = mm(B[3][rows(j), tokens_of(j // 2)], U[:, 4 * g + j, HD:128], X[:, j, 128:256],
                              start=True, stop=True)
                last.then_inc(pe_outq, 1)

            def phi(half):
                if half == 0:
                    pe.wait_ge(act_out, NG)
                else:
                    pe.wait_ge(pe_phi, 1)
                for c in range(1 + 3 * half, 4 + 3 * half):
                    r = slice(CH * (c % 4), CH * (c % 4) + CH)
                    for h in range(NH):
                        o = 256 * ((c - 1) // 3) + 64 * (h // 2)
                        last = mm(B[(c - 1) % 3][rows(h), o:o + 64], U[r, NH * (c // 4) + h, HD:128],
                                  btok[r, c // 4, cols(h)], start=True, stop=True)
                last.then_inc(pe_phi, 1)

            def psi(c):
                if c == 0:
                    pe.wait_ge(dve_q, NG)
                elif c == 1:
                    pe.wait_ge(act_phi, 1)
                else:
                    pe.wait_ge(dve_psi, c - 1)
                r = slice(CH * (c % 4), CH * (c % 4) + CH)
                for h in range(NH):
                    dst = B[3 - c % 2][rows(h), 64 * (h // 2):64 * (h // 2) + 64]
                    mm(dst, btok[r, c // 4, cols(h)], U[r, NH * (c // 4) + h, 0:HD], start=True, stop=False)
                    last = mm(dst, ktok[r, c // 4, cols(h)], vtok[r, c // 4, cols(h)], start=False, stop=True)
                last.then_inc(pe_psi, 1)

            def state(c):
                pe.wait_ge(act_phi, 1)
                if c == 1:
                    pe.wait_ge(dve_psi, 1)
                else:
                    pe.wait_ge(dve_state, c - 1)
                for h in range(NH):
                    last = mm(B[c % 2][rows(h), 64 * (h // 2):64 * (h // 2) + 64], PHI[rows(h), c - 1, h // 2, :],
                              states[rows(h), c - 1, h // 2, :], start=True, stop=True)
                last.then_inc(pe_state, 1)

            def states_out():
                pe.wait_ge(dve_state, NCH - 2)
                for h in range(NH):
                    for c in range(1, NCH):
                        o = T * ((h // 2) % 2) + CH * c
                        last = mm(B[h // 4][rows(h), o:o + CH], states[rows(h), c - 1, h // 2, :],
                                  s1[rows(h), h // 2, CH * c:CH * c + CH], start=True, stop=True)
                last.then_inc(pe_states_out, 1)

            def center():
                pe.wait_ge(dve_states_out, 1)
                by_pair((2, 3), lambda p: hblock[:, :], lambda p: s0[:, p, :], pe_mean)

            def deviation():
                pe.wait_ge(act_dev, 1)
                head_sums(s1, pe_var)

            def normalize():
                pe.wait_ge(dve_std, 1)
                by_pair((1, 2), lambda p: indT[:, p, :], lambda p: hsum[:, :], pe_norm)

            def gate():
                pe.wait_ge(gate_in, 16)
                by_pair((0, 3), lambda p: gate_up[:, tokens_of(p)], lambda p: zT[:, 13, :], pe_gate)

            def scores(who, h):
                if who == "x":
                    pe.wait_ge(out_taken, FIRST["xq"] + h + 1)
                elif h == 0:
                    pe.wait_ge(out_taken, FIRST["mq"] + 4)
                no = head_no(who, h)
                if no:
                    pe.wait_ge(dve_scores, no)
                if no >= 2:
                    pe.wait_ge(act_values, no - 1)
                    pe.wait_ge(dve_values, no - 1)
                for n in range(NT):
                    dst = B[4][:, 256 * n:256 * n + 256]
                    if who == "m":
                        keys = reach(who, n)
                        last = mm(dst[:, 0:keys], mqk[rows(h), h // 2, tokens_of(n)], mqk[rows(h), 4 + h // 2, 0:keys],
                                  start=True, stop=True)
                        continue
                    for a in range(2):
                        last = mm(dst, xqT[:, 2 * h + a, tokens_of(n)], xkey[:, 2 * h + a, :],
                                  start=(a == 0), stop=(a == 1))
                last.then_inc(pe_scores, 1)

            def turn(who, h):
                no = head_no(who, h)
                pe.wait_ge(dve_prob, no + 1)
                pe.wait_ge(*bank5[0])
                tiles = [(0, 0), (0, 1), (1, 1)] if who == "m" else [(0, 0), (0, 1), (1, 0), (1, 1)]
                for i, (k, n) in enumerate(tiles):
                    last = turn_op(B[5][:, tokens_of(i)], prob[:, n, tokens_of(k)], ident[:, :])
                last.then_inc(pe_turn, 1)
                bank5[0] = act_turn, no + 1

            def values(who, h):
                no = head_no(who, h)
                pe.wait_ge(act_turn, no + 1)
                pe.wait_ge(dve_scores, min(no + 2, NH if who == "m" else NH + XH))
                if no:
                    pe.wait_ge(dve_values, no)
                if who == "m":
                    if h == 0:
                        pe.wait_ge(out_taken, FIRST["mv"] + 2)
                    mm(B[4][rows(h), 0:256], mval[:, 0, cols(h)], probT[:, 0, :], start=True, stop=False)
                    last = mm(B[4][rows(h), 128:256], mval[:, 1, cols(h)], probT[:, 1, 0:128], start=False, stop=True)
                else:
                    pe.wait_ge(out_taken, KIND["xv"][h] + 1)
                    for a in range(2):
                        for k in range(2):
                            c = XD * h + 128 * a
                            last = mm(B[4][:, 256 * a:256 * a + 256], xval[:, k, c:c + 128], probT[:, k, :],
                                      start=(k == 0), stop=(k == 1))
                last.then_inc(pe_values, 1)

            in_order(Parts(dense, lambda: at[0], params=params, load=load, rms=rms, spread=spread, lora=lora, key_sums=key_sums,
                           keys=keys, bonus=bonus, tokens=tokens, mats=mats, nmat=nmat, pow2=pow2, pow4=pow4,
                           pow8=pow8, sides=sides, solve=solve, carry=carry, solved=solved, outq=outq, phi=phi,
                           psi=psi, state=state, states_out=states_out, center=center, deviation=deviation,
                           normalize=normalize, gate=gate, scores=scores, turn=turn, values=values))

        @block.scalar
        def _(act):
            op = nc.scalar.activation
            act.wait_ge(pool_const, 1)
            op(small[:, 15:16], eps[:, 0:1], ACT.Sqrt)
            at, links = [0], [0]

            def link(ins):
                links[0] += 1
                ins.then_inc(act_link, 1)
                act.wait_ge(act_link, links[0])

            def split_hi(s):
                u = s // 2
                act.wait_ge(raw_in[u % NRAW], 16 * (u // NRAW + 1))
                if s >= NSPLIT:
                    act.wait_ge(dense_mm, s - NSPLIT + 1)
                r, view = split_views(s)
                op(view(w_hi), r, ACT.Copy).then_inc(hi_done, 1)

            def quarter(q):
                if q % 2 == 0 and q // 2 + 2 < 2 * len(UNITS):
                    split_hi(q // 2 + 2)
                if q in AFTER:
                    follow(AFTER[q])

            def follow(o):
                what, j = OUTS[o][3:5]
                if what == "z":
                    act.wait_ge(dve_params, 2)
                    act.wait_ge(out_taken, o + 1)
                    for a in range(2):
                        t = 2 * j + a
                        last = op(zT[:, t, :], tmp[:, 0, a * T:a * T + T], ACT.Copy, scale=onemu[:, t:t + 1])
                    last.then_inc(act_rest, 1)
                if what == "xo":
                    operand(what, j)
                if what == "f1":
                    hidden(o)
                if what == "f2" and o >= len(OUTS) - 4:
                    final_square(o)

            def dense(n):
                for q in range(at[0], at[0] + n):
                    quarter(q)
                at[0] += n

            def operand(what, j):
                act.wait_ge(out_taken, FIRST[what] + j + 1)
                if what == "mix":
                    act.wait_ge(dense_mm, OUTS[LAST["mix"]][2] + 1)
                name = {"mix": "norm_xattn", "xo": "norm_ffn"}[what]
                for a in range(2):
                    last = op(op_hi[0][:, 2 * j + a, :], hT[:, 2 * j + a, :], ACT.Copy, scale=gain(name, 2 * j + a))
                last.then_inc(act_op, 1)

            def final_square(o):
                n = o - len(OUTS) + 4
                act.wait_ge(out_taken, o + 1)
                if n:
                    act.wait_ge(pe_square, 2 + n)
                else:
                    act.wait_ge(dve_hidden, 2 * NF)
                j = OUTS[o][4]
                op(pair(tmp[:, 1, :]), hT[:, 2 * j:2 * j + 2, :], ACT.Square).then_inc(act_square, 1)

            def hidden(o):
                n = nth(o)
                act.wait_ge(out_taken, o + 1)
                if n:
                    act.wait_ge(dve_hidden, n)
                k = 4 * (n // 2 % 2) + 2 * (n % 2)
                t = pair(tmp[:, 1, :])
                link(op(t, pair(tmp[:, 0, :]), ACT.Relu))
                link(op(t, t, ACT.Square))
                op(op_hi[1][:, k:k + 2, :], t, ACT.Copy).then_inc(act_hidden, 1)

            def load(m, q):
                n = 4 * m + q
                if m == 0:
                    act.wait_ge(dve_copy, q + 1)
                    if q == 0:
                        act.wait_ge(dve_params, 1)
                else:
                    act.wait_ge(pe_load, n + 1)
                src = hT[:, 2 * q:2 * q + 2, :] if m == 0 else pair(load_bank(m, q)[:, :])
                for a in range(2):
                    last = op(op_hi[m][:, 2 * q + a, :], src[:, a, :], ACT.Copy,
                              scale=gain(("norm_mix", "norm_mem")[m], 2 * q + a))
                last.then_inc(act_op, 1)
                if m == 0 and q % 2:
                    split_hi(q // 2)

            def stats(m):
                if m == 0:
                    act.wait_ge(x_in[0], 16)
                    act.wait_ge(x_in[1], 16)
                else:
                    act.wait_ge(mem_in, 16)
                    act.wait_ge(act_sums, 1)
                for n in range(NT):
                    last = op(sq_out, stage[m][:, n, :], ACT.Square, accum_out=row_sum[:, 2 * m + n:2 * m + n + 1])
                    if n == 0:
                        link(last)
                last.then_inc(act_sums, 1)
                act.wait_ge(act_sums, m + 1)
                r = row_sum[:, 2 * m:2 * m + 2]
                op(r, r, ACT.Sqrt, scale=1.0 / D, bias=eps[:, 0:1]).then_inc(act_root, 1)

            def rms(i):
                act.wait_ge(pe_square, i - 1)
                act.wait_ge(out_taken, FIRST[{2: "mix", 3: "xo"}[i]] + 4)
                op(rinv[:, 0, :], B[5][:, 0:T], ACT.Sqrt, bias=eps[:, 0:1]).then_inc(act_rms, 1)

            def gates():
                act.wait_ge(dve_shift, 1)
                op(zT[:, 13, :], zT[:, 13, :], ACT.Sigmoid)
                op(zT[0:64, 12, :], zT[0:64, 12, :], ACT.Tanh).then_inc(act_gates, 1)

            def rates():
                act.wait_ge(pe_lora, 1)
                for dst, b, name in ((s0, 0, "rwkv_w0"), (s3, 2, "rwkv_a0")):
                    for p in range(NP):
                        last = op(dst[:, p, :], B[b + p // 2][:, (p % 2) * T:(p % 2) * T + T], ACT.Sigmoid,
                                  bias=gain(name, p))
                last.then_inc(act_lora, 1)

            def decays():
                act.wait_ge(dve_sums, 1)
                op(s2[:, :, :], s1[:, :, :], ACT.Exp, scale=-DECAY)
                op(s0[:, :, :], s0[:, :, :], ACT.Exp, scale=-DECAY)
                op(s1[:, :, :], s1[:, :, :], ACT.Exp, scale=DECAY).then_inc(act_exp, 1)

            def key_sums():
                act.wait_ge(dve_shift, 3)
                for p in range(NP):
                    last = op(s4[:, p, :], zT[:, 4 + p, :], ACT.Square, scale=gain("rwkv_k_k", p))
                last.then_inc(act_kk, 1)

            def key_norm():
                act.wait_ge(dve_kk, 1)
                op(hsum[:, :], hsum[:, :], ACT.Sqrt).then_inc(act_kkroot, 1)

            def keys(step):
                if step == 2:
                    act.wait_ge(dve_A, 1)
                    for p in range(NP):
                        last = op(s0[:, p, :], s3[:, p, :], ACT.Identity, scale=gain("rwkv_k_a", p), bias=one_k_a[:, p:p + 1])
                    last.then_inc(act_factor, 1)

            def tokens():
                act.wait_ge(pe_btok, 1)
                op(btok[:, 0, :], B[0][:, :], ACT.Copy)
                op(btok[:, 1, :], B[1][:, :], ACT.Copy).then_inc(act_btok, 1)

            def bonus():
                act.wait_ge(pe_vtok, 1)
                act.wait_ge(dve_reads, 1)
                op(vtok[:, 0, :], B[1][:, :], ACT.Copy)
                op(vtok[:, 1, :], B[2][:, :], ACT.Copy).then_inc(act_vtok, 1)

            def pow2(g):
                act.wait_ge(pe_pow2, g + 1)
                op(neu[:, 2, :, :], quad(B[2][:, :]), ACT.Copy).then_inc(act_pow2, 1)

            def pow4(g):
                act.wait_ge(pe_pow4, g + 1)
                op(neu[:, 0, :, :], quad(B[0][:, :]), ACT.Copy)
                op(neu[:, 1, :, :], quad(B[1][:, :]), ACT.Copy).then_inc(act_pow4, 1)

            def pow8(g):
                act.wait_ge(pe_pow8, g + 1)
                op(neu[:, 2, :, :], quad(B[3][:, :]), ACT.Copy).then_inc(act_pow8, 1)

            def sides(g):
                act.wait_ge(pe_sides, g + 1)
                op(neu[:, 3, :, :], quad(B[2][:, :]), ACT.Copy).then_inc(act_sides, 1)

            def solve(g):
                act.wait_ge(pe_solve, g + 1)
                op(neu[:, 0, :, :], quad(B[3][:, :]), ACT.Copy).then_inc(act_solve, 1)

            def carry(g):
                act.wait_ge(pe_carry, g + 1)
                op(neu[:, 1, :, :], quad(B[0][:, :]), ACT.Copy).then_inc(act_carry, 1)

            def outq(g):
                act.wait_ge(pe_outq, g + 1)
                n, p = g // 2, 2 * (g % 2)
                op(s0[:, p:p + 2, tokens_of(n)], pair(B[2][:, 0:256]), ACT.Copy).then_inc(act_out, 1)

            def phi(half):
                if half == 0:
                    return
                act.wait_ge(pe_phi, 2)
                for b in range(3):
                    for c in range(2):
                        last = op(PHI[:, 3 * c + b, :, :].rearrange("p h k -> p (h k)"),
                                  B[b][:, 256 * c:256 * c + 256], ACT.Copy)
                last.then_inc(act_phi, 1)

            def deviation():
                act.wait_ge(dve_center, 1)
                op(s1[:, :, :], s0[:, :, :], ACT.Square).then_inc(act_dev, 1)
                act.wait_ge(pe_var, 1)
                op(hsum[:, :], B[0][0:8, 0:T], ACT.Sqrt, scale=1.0 / HD, bias=eps[0:8, 1:2]).then_inc(act_std, 1)

            def gate():
                for b in range(2):
                    act.wait_ge(dve_gate, b + 1)
                    op(op_hi[0][:, 2 * b:2 * b + 2, :], s0[:, 2 * b:2 * b + 2, :], ACT.Copy).then_inc(act_gate, 1)

            def scores(who, h):
                act.wait_ge(dve_scores, head_no(who, h) + 1)
                for n in range(NT):
                    p = prob[:, n, 0:reach(who, n)]
                    last = op(p, p, ACT.Exp, bias=small[:, n:n + 1],
                              accum_out=small[:, 2 + n:3 + n])
                last.then_inc(act_prob, 1)

            def turn(who, h):
                act.wait_ge(pe_turn, head_no(who, h) + 1)
                n = 384 if who == "m" else 512
                op(flat(probT[:, :, :])[:, 0:n], B[5][:, 0:n], ACT.Copy).then_inc(act_turn, 1)

            def values(who, h):
                act.wait_ge(pe_values, head_no(who, h) + 1)
                if who == "m":
                    dst, src = op_hi[0][rows(h), 4 + h // 2, :], B[4][rows(h), 0:T]
                else:
                    dst, src = op_hi[1][:, 2 * h:2 * h + 2, :], pair(B[4][:, :])
                op(dst, src, ACT.Copy).then_inc(act_values, 1)

            def final_rms():
                act.wait_ge(pe_square, 6)
                for n in range(NT):
                    last = op(row_sum[:, n:n + 1], B[4 + n][:, 0:1], ACT.Sqrt, bias=eps[:, 0:1])
                last.then_inc(act_root, 1)

            def finish():
                act.wait_ge(dve_rms, 5)
                act.wait_ge(pe_final, 4)
                for q in range(2):
                    for n in range(NT):
                        last = op(ostage[:, n, 256 * q:256 * q + 256], B[q][:, 256 * n:256 * n + 256], ACT.Copy,
                                  scale=row_sum[:, n:n + 1])
                    last.then_inc(act_final, 1)

            in_order(Parts(dense, lambda: at[0], load=load, stats=stats, rms=rms, gates=gates, rates=rates, operand=operand,
                           decays=decays, key_sums=key_sums, key_norm=key_norm, keys=keys, bonus=bonus,
                           tokens=tokens, pow2=pow2, pow4=pow4, pow8=pow8, sides=sides, solve=solve, carry=carry,
                           outq=outq, phi=phi, deviation=deviation, gate=gate, scores=scores, turn=turn,
                           values=values, final_rms=final_rms, finish=finish))

        @block.vector
        def _(dve):
            tt, ts, stt, cp = (nc.vector.tensor_tensor, nc.vector.tensor_scalar,
                               nc.vector.scalar_tensor_tensor, nc.vector.tensor_copy)
            dve.wait_ge(pool_const, 1)
            at, links = [0], [0]

            def link(ins):
                links[0] += 1
                ins.then_inc(dve_link, 1)
                dve.wait_ge(dve_link, links[0])

            def split_lo(s):
                dve.wait_ge(hi_done, s + 1)
                r, view = split_views(s)
                tt(view(w_lo), r, view(w_hi).bitcast(f32), ALU.subtract).then_inc(lo_done, 1)

            def quarter(q):
                if q % 2 == 0 and q // 2 + 2 < 2 * len(UNITS) and q // 2 + 2 not in POOL_SPLITS:
                    split_lo(q // 2 + 2)
                if q in AFTER and q not in ENDS:
                    follow(AFTER[q])
                if q in ENDS:
                    take(ENDS[q], *OUTS[ENDS[q]][3:5])
                    if AFTER.get(q) == ENDS[q]:
                        follow(ENDS[q])

            def follow(o):
                what, j = OUTS[o][3:5]
                if what == "z":
                    shift(nth(o), j)
                if what == "xo":
                    operand(what, j)
                if what == "f1":
                    hidden(nth(o))
                if what == "f2" and o >= len(OUTS) - 4:
                    final_gain(o, j)

            def dense(n):
                for q in range(at[0], at[0] + n):
                    quarter(q)
                at[0] += n

            def take(o, what, j):
                dve.wait_ge(dense_mm, OUTS[o][2] + 1)
                src = pair(dense_bank[o % 2][:, :])
                if what in ("mix", "xo", "f2"):
                    h = hT[:, 2 * j:2 * j + 2, :]
                    if what == "xo":
                        dve.wait_ge(pool_square, 1)
                    if what == "f2" and o < FIRST["f2"] + 4:
                        dve.wait_ge(pool_square, 2)
                    dve.wait_ge(out_taken, o)
                    tt(h, src, h, ALU.add).then_inc(out_taken, 1)
                    return
                n = nth(o)
                if what == "z" and n:
                    dve.wait_ge(dve_shift, n)
                if what in ("mv", "xv"):
                    values_of, m = (mval, 0) if what == "mv" else (xval, 1)
                    for n in range(NT):
                        last = ts(values_of[:, n, 256 * j:256 * j + 256], dense_bank[o % 2][:, 256 * n:256 * n + 256],
                                  row_sum[:, 2 * m + n:2 * m + n + 1], None, ALU.mult)
                    last.then_inc(out_taken, 1)
                    return
                if what == "f1":
                    if n:
                        dve.wait_ge(act_hidden, n)
                    else:
                        dve.wait_ge(dve_shift, 7)
                if what in ("z", "xk", "xv"):
                    dve.wait_ge(dve_rms, 2 if what in ("xk", "xv") else 1)
                if o == FIRST["xq"]:
                    dve.wait_ge(dve_rms, 3)
                    dve.wait_ge(act_values, NH)
                if o == FIRST["f1"]:
                    dve.wait_ge(dve_rms, 4)
                dst = {"mq": mqk, "xk": xkey, "xq": xqT}.get(what)
                dst = pair(tmp[:, 0, :]) if dst is None else dst[:, 2 * j:2 * j + 2, :]
                r = 1 if what in ("xk", "xv") else 0
                tt(dst, src, rinv[:, r:r + 1, :].to_broadcast([128, 2, T]), ALU.mult).then_inc(out_taken, 1)

            def shift(n, j):
                dve.wait_ge(act_rest, n + 1)
                for a in range(2):
                    t = 2 * j + a
                    last = stt(out=zT[:, t, 1:T], in0=tmp[:, 0, a * T:a * T + T - 1], scalar=gain("rwkv_mu", t),
                               in1=zT[:, t, 1:T], op0=ALU.mult, op1=ALU.add)
                last.then_inc(dve_shift, 1)

            def operand(what, j):
                dve.wait_ge(act_op, op_no(what, j) + 1)
                name = {"mix": "norm_xattn", "xo": "norm_ffn"}[what]
                for a in range(2):
                    k = 2 * j + a
                    last = stt(out=op_lo[0][:, k, :], in0=hT[:, k, :], scalar=gain(name, k),
                               in1=op_hi[0][:, k, :].bitcast(f32), op0=ALU.mult, op1=ALU.subtract)
                last.then_inc(dve_op, 1)

            def final_gain(o, j):
                dve.wait_ge(out_taken, o + 1)
                for k in (2 * j, 2 * j + 1):
                    last = ts(zT[:, k, :], hT[:, k, :], gain("norm_final", k), None, ALU.mult)
                last.then_inc(dve_gain, 1)

            def hidden(n):
                dve.wait_ge(act_hidden, n + 1)
                k = 4 * (n // 2 % 2) + 2 * (n % 2)
                tt(op_lo[1][:, k:k + 2, :], pair(tmp[:, 1, :]), op_hi[1][:, k:k + 2, :].bitcast(f32),
                   ALU.subtract).then_inc(dve_hidden, 1)

            def params(part):
                dve.wait_ge(pe_params, part + 1)
                if part == 0:
                    cp(par[:, 0:8], B[4][:, 0:8]).then_inc(dve_params, 1)
                    return
                link(cp(par[:, 8:NROW], B[4][:, 8:NROW]))
                r = ROW["rwkv_mu"][0]
                ts(onemu[:, :], par[:, r:r + 14], -1.0, 1.0, ALU.mult, ALU.add)
                r = ROW["rwkv_k_a"][0]
                ts(one_k_a[:, :], par[:, r:r + NP], -1.0, 1.0, ALU.mult, ALU.add).then_inc(dve_params, 1)
                dve.wait_ge(dve_params, 2)

            def load(m, q):
                if m == 0:
                    for c in ((0, 1), (2,), (3,), ())[q]:
                        dve.wait_ge(pe_load, c + 1)
                        cp(hT[:, 2 * c:2 * c + 2, :], pair(B[c][:, :])).then_inc(dve_copy, 1)
                    dve.wait_ge(dve_copy, q + 1)
                    dve.wait_ge(dve_params, 1)
                elif q == 0:
                    dve.wait_ge(dve_params, 2)
                dve.wait_ge(act_op, 4 * m + q + 1)
                src = hT[:, 2 * q:2 * q + 2, :] if m == 0 else pair(load_bank(m, q)[:, :])
                for a in range(2):
                    k = 2 * q + a
                    last = stt(out=op_lo[m][:, k, :], in0=src[:, a, :], scalar=gain(("norm_mix", "norm_mem")[m], k),
                               in1=op_hi[m][:, k, :].bitcast(f32), op0=ALU.mult, op1=ALU.subtract)
                last.then_inc(dve_op, 1)
                if m == 0 and q % 2:
                    split_lo(q // 2)

            def diagonal_of(m):
                dve.wait_ge(act_root, m + 1)
                r = row_sum[:, 2 * m:2 * m + 2]
                link(nc.vector.reciprocal(r, r))
                for n in range(NT):
                    last = ts(diagonal[m][:, n, :], ident[:, :], row_sum[:, 2 * m + n:2 * m + n + 1], float(D), ALU.mult, ALU.mult)
                last.then_inc(dve_diag, 1)

            def spread(m):
                dve.wait_ge(pe_spread_rms, m + 1)
                cp(rinv[:, m, :], B[5][:, 0:T]).then_inc(dve_rms, 1)

            def rms(i):
                dve.wait_ge(act_rms, i - 1)
                nc.vector.reciprocal(rinv[:, 0, :], rinv[:, 0, :]).then_inc(dve_rms, 1)

            def sums():
                dve.wait_ge(act_lora, 1)
                dve.wait_ge(pool_const, 2)
                link(nc.vector.tensor_tensor_scan(out=flat(s1[:, :, :]), data0=reset, data1=flat(s0[:, :, :]),
                                                  initial=0.0, op0=ALU.mult, op1=ALU.add))
                tt(s0[:, :, :], s1[:, :, :], s0[:, :, :], ALU.subtract).then_inc(dve_sums, 1)

            def key_norm():
                dve.wait_ge(pe_kk, 1)
                ts(hsum[:, :], B[0][0:8, 0:T], 1e-24, None, ALU.max).then_inc(dve_kk, 1)
                dve.wait_ge(act_kkroot, 1)
                nc.vector.reciprocal(hsum[:, :], hsum[:, :]).then_inc(dve_kkinv, 1)

            def keys(step):
                kz, kk, rate, p_inv = flat(zT[:, 4:8, :]), flat(s4[:, :, :]), flat(s3[:, :, :]), flat(s1[:, :, :])
                q = lambda x: x[:, :, :].rearrange("p a (n t) -> p (a n) t", n=NT)
                if step == 0:
                    dve.wait_ge(pe_spread, 1)
                    for p in range(NP):
                        last = stt(out=s4[:, p, :], in0=zT[:, 4 + p, :], scalar=gain("rwkv_k_k", p),
                                   in1=B[1 + p // 2][:, (p % 2) * T:(p % 2) * T + T], op0=ALU.mult, op1=ALU.mult)
                    last.then_inc(dve_kk_all, 1)
                if step == 1:
                    dve.wait_ge(dve_kk_all, 1)
                    dve.wait_ge(act_exp, 1)
                    cp(pend[:, :, :], s2[:, :, CH - 1::CH])
                    stt(out=AR[:, :, :, 0, :].rearrange("p a n t -> p (a n) t"), in0=q(s4), scalar=-1.0,
                        in1=q(s0), op0=ALU.mult, op1=ALU.mult).then_inc(dve_A, 1)
                if step == 2:
                    dve.wait_ge(act_factor, 1)
                    link(tt(rate, kk, rate, ALU.mult))
                    tt(rate, rate, p_inv, ALU.mult).then_inc(dve_B, 1)
                if step == 3:
                    dve.wait_ge(dve_B, 1)
                    link(tt(kz, flat(s0[:, :, :]), kz, ALU.mult))
                    tt(kk, kz, p_inv, ALU.mult).then_inc(dve_keys, 1)

            def reads():
                dve.wait_ge(dve_shift, 5)
                dve.wait_ge(pool_R, 1)
                for p in range(NP):
                    last = stt(out=s2[:, p, :], in0=zT[:, p, :], scalar=gain("rwkv_r_k", p), in1=zT[:, 4 + p, :],
                               op0=ALU.mult, op1=ALU.mult)
                last.then_inc(dve_reads, 1)

            def bonus():
                dve.wait_ge(pe_bonus, 1)
                for a, b in ((0, 3), (2, 0)):
                    last = stt(out=s2[:, a:a + 2, :], in0=pair(B[b][:, :]), scalar=float(HD), in1=zT[:, 8 + a:10 + a, :],
                               op0=ALU.mult, op1=ALU.mult)
                last.then_inc(dve_bonus, 1)

            def tokens():
                dve.wait_ge(pe_btok, 1)
                dve.wait_ge(dve_reads, 1)
                cp(ktok[:, 0, :], B[2][:, :])
                cp(ktok[:, 1, :], B[3][:, :]).then_inc(dve_ktok, 1)

            def mats(g):
                dve.wait_ge(pe_mats, g + 1)
                for half in range(2):
                    for j in (2 * half, 2 * half + 1):
                        tt(quad(X[:, j, :]), quad(B[j][:, :]), maskX[:, :, :], ALU.mult)
                        last = tt(neu[:, 0, j, :], B[j][:, 0:128], mask_d[:, :], ALU.mult)
                    last.then_inc(dve_mats, 1)

            def nmat(g):
                dve.wait_ge(dve_mats, 2 * g + 2)
                tt(neu[:, 4, :, :], neu[:, 0, :, :], ident[:, :].unsqueeze(1).to_broadcast([128, 4, 128]), ALU.add)
                dve.wait_ge(pe_nmat, g + 1)
                for b in range(2):
                    last = tt(neu[:, 1, b::2, :], pair(B[b][:, 0:256]),
                              mask_n[:, :].unsqueeze(1).to_broadcast([128, 2, 128]), ALU.mult)
                last.then_inc(dve_nmat, 1)

            def pow2(g):
                dve.wait_ge(pe_pow2, g + 1)
                cp(neu[:, 3, :, :], quad(B[3][:, :])).then_inc(dve_pow2, 1)

            def pow4(g):
                dve.wait_ge(pe_pow4, g + 1)
                tt(neu[:, 4, :, :], quad(B[2][:, :]), neu[:, 4, :, :], ALU.add).then_inc(dve_pow4, 1)

            def pow8(g):
                dve.wait_ge(pe_pow8, g + 1)
                tt(neu[:, 4, :, :], quad(B[0][:, :]), neu[:, 4, :, :], ALU.add).then_inc(dve_pow8, 1)

            def sides(g):
                dve.wait_ge(pe_sides, g + 1)
                tt(neu[:, 4, :, :], quad(B[1][:, :]), neu[:, 4, :, :], ALU.add).then_inc(dve_inverse, 1)

            def solved(g):
                dve.wait_ge(pe_solved, g + 1)
                tt(U[:, 4 * g:4 * g + 4, :], quad(B[1][:, :]), neu[:, 0, :, :], ALU.add).then_inc(dve_solved, 1)

            def outq(g):
                dve.wait_ge(pe_outq, g + 1)
                n, p = g // 2, 2 * (g % 2)
                tt(s1[:, p:p + 2, tokens_of(n)], pair(B[3][:, 0:256]), AR[:, p:p + 2, n, 1, :], ALU.add).then_inc(dve_q, 1)

            def phi(half):
                if half == 0:
                    for p in range(NP):
                        ts(s2[:, p, :], s2[:, p, :], gain("rwkv_ln_b", p), None, ALU.add).then_inc(dve_ln_b, 1)

            def from_bank(b):
                return B[b][:, 0:256].rearrange("p (h v) -> p h v", h=NP)

            def psi(c):
                if c:
                    dve.wait_ge(dve_psi, c)
                    if c > 1:
                        dve.wait_ge(dve_state, c - 1)
                    link(tt(s4[:, :, 0:HD], states[:, c - 1, :, :], pend[:, :, c:c + 1].to_broadcast([128, NP, HD]), ALU.mult))
                dve.wait_ge(pe_psi, c + 1)
                if c == 0:
                    cp(states[:, 0, :, :], from_bank(3)).then_inc(dve_psi, 1)
                else:
                    tt(s4[:, :, 0:HD], from_bank(3 - c % 2), s4[:, :, 0:HD], ALU.add).then_inc(dve_psi, 1)

            def state(c):
                dve.wait_ge(dve_psi, c + 1)
                dve.wait_ge(pe_state, c)
                tt(states[:, c, :, :], from_bank(c % 2), s4[:, :, 0:HD], ALU.add).then_inc(dve_state, 1)

            def states_out():
                dve.wait_ge(pe_states_out, 1)
                for b in range(2):
                    y = s0[:, 2 * b:2 * b + 2, CH:T]
                    last = tt(y, pair(B[b][:, :])[:, :, CH:T], y, ALU.add)
                last.then_inc(dve_states_out, 1)

            def center():
                dve.wait_ge(dve_states_out, 1)
                dve.wait_ge(pe_mean, 1)
                for b in range(2):
                    y = s0[:, 2 * b:2 * b + 2, :]
                    last = stt(out=y, in0=pair(B[2 + b][:, :]), scalar=-1.0, in1=y, op0=ALU.mult, op1=ALU.add)
                last.then_inc(dve_center, 1)

            def deviation():
                dve.wait_ge(act_std, 1)
                nc.vector.reciprocal(hsum[:, :], hsum[:, :]).then_inc(dve_std, 1)

            def normalize():
                dve.wait_ge(pe_norm, 1)
                dve.wait_ge(dve_ln_b, NP)
                for p in range(NP):
                    last = stt(out=s0[:, p, :], in0=B[1 + p // 2][:, (p % 2) * T:(p % 2) * T + T],
                               scalar=gain("rwkv_ln_w", p), in1=s0[:, p, :], op0=ALU.mult, op1=ALU.mult)
                link(last)
                tt(s0[:, :, :], s0[:, :, :], s2[:, :, :], ALU.add).then_inc(dve_norm, 1)

            def gate():
                dve.wait_ge(dve_norm, 1)
                dve.wait_ge(pe_gate, 1)
                for b in range(2):
                    y = s0[:, 2 * b:2 * b + 2, :]
                    tt(y, pair(B[(0, 3)[b]][:, :]), y, ALU.mult).then_inc(dve_gate, 1)
                for b in range(2):
                    dve.wait_ge(act_gate, b + 1)
                    tt(op_lo[0][:, 2 * b:2 * b + 2, :], s0[:, 2 * b:2 * b + 2, :],
                       op_hi[0][:, 2 * b:2 * b + 2, :].bitcast(f32), ALU.subtract).then_inc(dve_gate, 1)

            def scores(who, h):
                no = head_no(who, h)
                dve.wait_ge(pe_scores, no + 1)
                if no:
                    dve.wait_ge(pe_turn, no)
                if who == "m":
                    for n in range(NT):
                        keys = reach(who, n)
                        last = stt(out=prob[:, n, 0:keys], in0=B[4][:, 256 * n:256 * n + keys], scalar=HD ** -0.5,
                                   in1=causal[:, n, 0:keys], op0=ALU.mult, op1=ALU.add)
                    link(last)
                    for n in range(NT):
                        last = nc.vector.reduce_max(small[:, n:n + 1], prob[:, n, 0:reach(who, n)], AX.X, negate=True)
                    last.then_inc(dve_scores, 1)
                else:
                    link(ts(prob[:, :, :], pair(B[4][:, :]), XD ** -0.5, None, ALU.mult))
                    nc.vector.reduce_max(small[:, 0:2], prob[:, :, :], AX.X, negate=True).then_inc(dve_scores, 1)

            def weigh(who, h):
                dve.wait_ge(act_prob, head_no(who, h) + 1)
                link(nc.vector.reciprocal(small[:, 4:6], small[:, 2:4]))
                for n in range(NT):
                    p = prob[:, n, 0:reach(who, n)]
                    last = ts(p, p, small[:, 4 + n:5 + n], None, ALU.mult)
                last.then_inc(dve_prob, 1)

            def values(who, h):
                dve.wait_ge(act_values, head_no(who, h) + 1)
                if who == "m":
                    r, k = rows(h), 4 + h // 2
                    tt(op_lo[0][r, k, :], B[4][r, 0:T], op_hi[0][r, k, :].bitcast(f32), ALU.subtract).then_inc(dve_values, 1)
                else:
                    k = slice(2 * h, 2 * h + 2)
                    tt(op_lo[1][:, k, :], pair(B[4][:, :]), op_hi[1][:, k, :].bitcast(f32), ALU.subtract)\
                        .then_inc(dve_values, 1)

            def final_rms():
                dve.wait_ge(act_root, 3)
                nc.vector.reciprocal(row_sum[:, 0:2], row_sum[:, 0:2]).then_inc(dve_rms, 1)

            def finish():
                dve.wait_ge(dve_rms, 5)
                dve.wait_ge(pe_final, 4)
                for q in range(2, 4):
                    for n in range(NT):
                        last = ts(ostage[:, n, 256 * q:256 * q + 256], B[q][:, 256 * n:256 * n + 256],
                                  row_sum[:, n:n + 1], None, ALU.mult)
                    last.then_inc(dve_final, 1)

            in_order(Parts(dense, lambda: at[0], params=params, load=load, diagonal=diagonal_of, spread=spread, rms=rms,
                           operand=operand, sums=sums, key_norm=key_norm,
                           keys=keys, reads=reads, bonus=bonus, tokens=tokens, mats=mats, nmat=nmat, pow2=pow2,
                           pow4=pow4, pow8=pow8, sides=sides, solved=solved, outq=outq, phi=phi, psi=psi, state=state,
                           states_out=states_out, center=center, deviation=deviation, normalize=normalize, gate=gate,
                           scores=scores, weigh=weigh, values=values, final_rms=final_rms, finish=finish))


INPUTS = ["x", "mem", "norm_mix", "w_in", "rwkv_mu", "rwkv_w0", "rwkv_w_up", "rwkv_a0", "rwkv_a_up", "rwkv_g_up",
          "rwkv_k_k", "rwkv_k_a", "rwkv_r_k", "rwkv_ln_w", "rwkv_ln_b", "w_mix_out", "norm_xattn", "norm_mem",
          "w_xq", "w_xkv", "w_xo", "norm_ffn", "w_ff1", "w_ff2", "norm_final"]


def kernel(**inputs):
    import numpy as np
    import concourse.bacc as bacc
    from concourse.bass_utils import run_bass_kernel_spmd

    nc = bacc.Bacc("TRN2", target_bir_lowering=False, num_devices=1)
    arrays, io = {}, {}
    for name in INPUTS:
        a = np.ascontiguousarray(inputs[name])
        arrays[f"in_{name}"] = a
        io[name] = nc.dram_tensor(f"in_{name}", a.shape, mybir.dt.from_np(a.dtype), kind="ExternalInput").ap()
    out = nc.dram_tensor("out", (1, T, D), mybir.dt.float32, kind="ExternalOutput").ap()
    build(nc, io, out)
    return run_bass_kernel_spmd(nc, [arrays], core_ids=[0]).results[0]["out"]
```
